# Optimizing a Trainium2 kernel written in Bass

```python
import math
import jax
import jax.numpy as jnp
from jax import lax
import numpy as np

D_MODEL = 1024
BATCH = 1
SEQ = 512
DEPTH = 2

N_MIXERS = 2
Q_BLOCK = 128
NORM_EPS = 1e-6
FOX_HEADS = 16
FOX_HEAD_DIM = D_MODEL // FOX_HEADS
FOX_WIDTH = FOX_HEADS * FOX_HEAD_DIM
MLA_HEADS = 16
MLA_NOPE_DIM = 64
MLA_ROPE_DIM = 32
MLA_V_DIM = 64
MLA_Q_RANK = 384
MLA_KV_RANK = 256
ROPE_BASE = 10000.0
D_FF = 2816
CONV_WIDTH = 3
N_FOX_LAYERS = (DEPTH + 1) // 2
N_MLA_LAYERS = DEPTH // 2

kernel_name = 'hybrid_fox_mla_convffn_adaln'

def rms_norm(x):
    xf = x.astype(jnp.float32)
    y = xf * lax.rsqrt(jnp.mean(xf * xf, axis=-1, keepdims=True) + NORM_EPS)
    return y.astype(x.dtype)

def ada_modulation(c, w, b):
    mod = jax.nn.silu(c) @ w + b
    shift, scale, gate = jnp.split(mod[:, None, :], 3, axis=-1)
    return shift, scale, gate

def causal_mask(start, seq):
    q_pos = start + jnp.arange(Q_BLOCK)
    return q_pos[:, None] >= jnp.arange(seq)[None, :]

def masked_softmax(s, mask):
    s = jnp.where(mask, s.astype(jnp.float32), -jnp.inf)
    return jax.nn.softmax(s, axis=-1)

def causal_block_sweep(block_fn, batch, seq):
    starts = jnp.arange(seq // Q_BLOCK, dtype=jnp.int32) * Q_BLOCK
    out = lax.map(block_fn, starts)
    return jnp.moveaxis(out, 0, 1).reshape(batch, seq, -1)

def forgetting_attention(h, w_in, b_f, w_o):
    B, S, _ = h.shape
    proj = h @ w_in
    q, k, v, f_logit = jnp.split(proj, [FOX_WIDTH, 2 * FOX_WIDTH, 3 * FOX_WIDTH], axis=-1)
    q = q.reshape(B, S, FOX_HEADS, FOX_HEAD_DIM)
    k = k.reshape(B, S, FOX_HEADS, FOX_HEAD_DIM)
    v = v.reshape(B, S, FOX_HEADS, FOX_HEAD_DIM)
    log_f = jax.nn.log_sigmoid((f_logit + b_f).astype(jnp.float32))
    cum = jnp.cumsum(log_f, axis=1).transpose(0, 2, 1)
    scale = FOX_HEAD_DIM ** -0.5

    def block(start):
        qb = lax.dynamic_slice_in_dim(q, start, Q_BLOCK, axis=1)
        cq = lax.dynamic_slice_in_dim(cum, start, Q_BLOCK, axis=2)
        s = jnp.einsum('bqhd,bkhd->bhqk', qb, k).astype(jnp.float32) * scale
        s = s + (cq[..., :, None] - cum[..., None, :])
        p = masked_softmax(s, causal_mask(start, S))
        return jnp.einsum('bhqk,bkhd->bqhd', p.astype(v.dtype), v)

    o = causal_block_sweep(block, B, S)
    return o @ w_o

def apply_rope(x, cos, sin):
    half = x.shape[-1] // 2
    x1, x2 = x[..., :half], x[..., half:]
    return jnp.concatenate([x1 * cos - x2 * sin, x2 * cos + x1 * sin], axis=-1)

def latent_attention(h, w_a, g_q, g_kv, w_uq, w_ukv, w_o):
    B, S, _ = h.shape
    a = h @ w_a
    c_q, c_kv, k_rope = jnp.split(a, [MLA_Q_RANK, MLA_Q_RANK + MLA_KV_RANK], axis=-1)
    c_q = rms_norm(c_q) * g_q
    c_kv = rms_norm(c_kv) * g_kv
    q = (c_q @ w_uq).reshape(B, S, MLA_HEADS, MLA_NOPE_DIM + MLA_ROPE_DIM)
    q_nope, q_rope = q[..., :MLA_NOPE_DIM], q[..., MLA_NOPE_DIM:]
    kv = (c_kv @ w_ukv).reshape(B, S, MLA_HEADS, MLA_NOPE_DIM + MLA_V_DIM)
    k_nope, v = kv[..., :MLA_NOPE_DIM], kv[..., MLA_NOPE_DIM:]

    pos = jnp.arange(S, dtype=jnp.float32)
    inv_freq = ROPE_BASE ** (-jnp.arange(0, MLA_ROPE_DIM, 2, dtype=jnp.float32) / MLA_ROPE_DIM)
    ang = pos[:, None] * inv_freq[None, :]
    cos = jnp.cos(ang).astype(h.dtype)
    sin = jnp.sin(ang).astype(h.dtype)
    q_rope = apply_rope(q_rope, cos[:, None, :], sin[:, None, :])
    k_rope = apply_rope(k_rope, cos, sin)
    scale = (MLA_NOPE_DIM + MLA_ROPE_DIM) ** -0.5

    def block(start):
        qn = lax.dynamic_slice_in_dim(q_nope, start, Q_BLOCK, axis=1)
        qr = lax.dynamic_slice_in_dim(q_rope, start, Q_BLOCK, axis=1)
        s = jnp.einsum('bqhd,bkhd->bhqk', qn, k_nope) + jnp.einsum('bqhr,bkr->bhqk', qr, k_rope)
        p = masked_softmax(s.astype(jnp.float32) * scale, causal_mask(start, S))
        return jnp.einsum('bhqk,bkhd->bqhd', p.astype(v.dtype), v)

    o = causal_block_sweep(block, B, S)
    return o @ w_o

def conv_gated_mlp(h, w_in, conv_w, conv_b, w_out):
    S = h.shape[1]
    u = h @ w_in
    u_pad = jnp.pad(u, ((0, 0), (CONV_WIDTH - 1, 0), (0, 0)))
    y = conv_b
    for j in range(CONV_WIDTH):
        y = y + conv_w[j] * u_pad[:, j:j + S, :]
    gate, val = jnp.split(y, 2, axis=-1)
    return (jax.nn.silu(gate) * val) @ w_out

def setup_inputs(seed: int = 0) -> dict:
    key = jax.random.key(seed)
    ks = jax.random.split(key, 20)
    D = D_MODEL
    nrm = jax.random.normal
    f32 = jnp.float32
    x = nrm(ks[0], (BATCH, SEQ, D), f32)
    c = nrm(ks[1], (BATCH, D), f32)
    ada_w = nrm(ks[2], (DEPTH, 2, D, 3 * D), f32) * D ** -0.5
    ada_b = 0.02 * nrm(ks[3], (DEPTH, 2, 3 * D), f32)
    fox_w_in = nrm(ks[4], (N_FOX_LAYERS, D, 3 * FOX_WIDTH + FOX_HEADS), f32) * D ** -0.5
    fox_w_in = fox_w_in.at[..., 3 * FOX_WIDTH:].multiply(0.1)
    fox_b_f = jnp.linspace(2.0, 6.0, FOX_HEADS, dtype=f32)[None, :] + 0.1 * nrm(ks[5], (N_FOX_LAYERS, FOX_HEADS), f32)
    fox_w_o = nrm(ks[6], (N_FOX_LAYERS, FOX_WIDTH, D), f32) * FOX_WIDTH ** -0.5
    mla_w_a = nrm(ks[7], (N_MLA_LAYERS, D, MLA_Q_RANK + MLA_KV_RANK + MLA_ROPE_DIM), f32) * D ** -0.5
    mla_g_q = 1.0 + 0.02 * nrm(ks[8], (N_MLA_LAYERS, MLA_Q_RANK), f32)
    mla_g_kv = 1.0 + 0.02 * nrm(ks[9], (N_MLA_LAYERS, MLA_KV_RANK), f32)
    mla_w_uq = nrm(ks[10], (N_MLA_LAYERS, MLA_Q_RANK, MLA_HEADS * (MLA_NOPE_DIM + MLA_ROPE_DIM)), f32) * MLA_Q_RANK ** -0.5
    mla_w_ukv = nrm(ks[11], (N_MLA_LAYERS, MLA_KV_RANK, MLA_HEADS * (MLA_NOPE_DIM + MLA_V_DIM)), f32) * MLA_KV_RANK ** -0.5
    mla_w_o = nrm(ks[12], (N_MLA_LAYERS, MLA_HEADS * MLA_V_DIM, D), f32) * (MLA_HEADS * MLA_V_DIM) ** -0.5
    ffn_w_in = nrm(ks[13], (DEPTH, D, 2 * D_FF), f32) * D ** -0.5
    ffn_conv_w = nrm(ks[14], (DEPTH, CONV_WIDTH, 2 * D_FF), f32) * CONV_WIDTH ** -0.5
    ffn_conv_b = 0.02 * nrm(ks[15], (DEPTH, 2 * D_FF), f32)
    ffn_w_out = nrm(ks[16], (DEPTH, D_FF, D), f32) * D_FF ** -0.5
    final_g = 1.0 + 0.02 * nrm(ks[17], (D,), f32)
    return {'x': x, 'c': c, 'ada_w': ada_w, 'ada_b': ada_b,
            'fox_w_in': fox_w_in, 'fox_b_f': fox_b_f, 'fox_w_o': fox_w_o,
            'mla_w_a': mla_w_a, 'mla_g_q': mla_g_q, 'mla_g_kv': mla_g_kv,
            'mla_w_uq': mla_w_uq, 'mla_w_ukv': mla_w_ukv, 'mla_w_o': mla_w_o,
            'ffn_w_in': ffn_w_in, 'ffn_conv_w': ffn_conv_w, 'ffn_conv_b': ffn_conv_b,
            'ffn_w_out': ffn_w_out, 'final_g': final_g}

def reference(x, c, ada_w, ada_b, fox_w_in, fox_b_f, fox_w_o, mla_w_a, mla_g_q, mla_g_kv,
              mla_w_uq, mla_w_ukv, mla_w_o, ffn_w_in, ffn_conv_w, ffn_conv_b, ffn_w_out, final_g):
    for i in range(DEPTH):
        j = i // N_MIXERS
        shift, scale, gate = ada_modulation(c, ada_w[i, 0], ada_b[i, 0])
        h = rms_norm(x) * (1.0 + scale) + shift
        if i % N_MIXERS == 0:
            y = forgetting_attention(h, fox_w_in[j], fox_b_f[j], fox_w_o[j])
        else:
            y = latent_attention(h, mla_w_a[j], mla_g_q[j], mla_g_kv[j],
                                 mla_w_uq[j], mla_w_ukv[j], mla_w_o[j])
        x = x + gate * y
        shift, scale, gate = ada_modulation(c, ada_w[i, 1], ada_b[i, 1])
        h = rms_norm(x) * (1.0 + scale) + shift
        x = x + gate * conv_gated_mlp(h, ffn_w_in[i], ffn_conv_w[i], ffn_conv_b[i], ffn_w_out[i])
    return rms_norm(x) * final_g


_drawn_inputs = setup_inputs


def setup_inputs(seed=0):
    import zlib

    import numpy as np

    out = dict(_drawn_inputs(seed))
    spreads = {}
    factors = {'mla_g_q': 8.0, 'mla_g_kv': 8.0, 'ffn_conv_b': 3.645, 'final_g': 2.886}
    for name, (base, spread) in spreads.items():
        noise = np.random.default_rng([zlib.crc32(name.encode()), seed]).standard_normal(out[name].shape)
        drawn = base * np.exp(spread * noise) if base else spread * noise
        out[name] = jnp.asarray(drawn.astype(out[name].dtype))
    for name, factor in factors.items():
        out[name] = (out[name] * factor).astype(out[name].dtype)
    return out
```

```python
from contextlib import ExitStack

import numpy as np

import concourse.bass as bass
from concourse import mybir

F32 = mybir.dt.float32
F32R = mybir.dt.float32r
BF16 = mybir.dt.bfloat16
ALU = mybir.AluOpType
ACT = mybir.ActivationFunctionType
AX = mybir.AxisListType

P = 128
D = 1024
DT = D // P
S = 512
QB = S // P
HEADS = 16
HD = 64
PAIRS = HEADS // 2
ROPE = 32
MQ = HD + ROPE
QR, KVR = 384, 256
QRT, KVRT = QR // P, KVR // P
FF = 2816
FFT = FF // P
DOWN_K = (8, 7, 7)
SUBS = 4
MODT = 3 * DT
EPS = 1e-6
FOX_SCALE = float(HD) ** -0.5
MLA_SCALE = float(MQ) ** -0.5
MASKED = -1.0e30

C_F = 0
C_FOX = 1
C_FOXO = C_FOX + 3 * PAIRS
C_UP0 = C_FOXO + DT
C_DOWN0 = C_UP0 + 2 * FFT
C_MA = C_DOWN0 + 3 * DT
C_MLA = C_MA + QRT + KVRT + 1
C_MLAO = C_MLA + 2 * HEADS
C_UP1 = C_MLAO + DT
C_DOWN1 = C_UP1 + 2 * FFT
C_END = C_DOWN1 + 3 * DT
C_UP, C_DOWN = (C_UP0, C_UP1), (C_DOWN0, C_DOWN1)
T_F = 0
T_FOX = 1
T_FOXO = T_FOX + 3 * PAIRS
T_UP0 = T_FOXO + DT
T_DOWN0 = T_UP0 + 2 * FFT
T_MA = T_DOWN0 + DT
T_MLA = T_MA + QRT + KVRT + 1
T_MLAO = T_MLA + 2 * HEADS
T_UP1 = T_MLAO + DT
T_DOWN1 = T_UP1 + 2 * FFT
T_UP, T_DOWN = (T_UP0, T_UP1), (T_DOWN0, T_DOWN1)
U_FOX, U_MLA = 0, HEADS * QB
H_FOX, H_MLA = 0, HEADS
FOX_TR = 2 * QB + 1
MLA_TR = QB + 1
R_FOX = 0
R_MLA = R_FOX + FOX_TR * PAIRS
N_SUB = (0, 1, 2, 5)
N_CQ, N_CKV, N_FINAL = 3, 4, 6
SSQ_TILES = (DT, DT, DT, QRT, KVRT, DT, DT)
SSQ_END = [sum(t + 1 for t in SSQ_TILES[:n + 1]) for n in range(len(SSQ_TILES))]
SQ_END = [sum(SSQ_TILES[:n + 1]) for n in range(len(SSQ_TILES))]
AG = 192
AGN = 3 * D // AG
AK = DT // 2
AH = 2 * AGN
V_C = 0
V_B = V_C + DT
V_GF = V_B + SUBS * MODT
V_GQ = V_GF + DT
V_GKV = V_GQ + QRT
V_ROWS = V_GKV + KVRT


def chunk_k(n):
    if C_MLA <= n < C_MLAO:
        return QRT if (n - C_MLA) % 2 == 0 else KVRT
    for base in C_DOWN:
        if base <= n < base + 3 * DT:
            return DOWN_K[(n - base) % 3]
    return DT


def slot_loads(n):
    if n == C_F:
        return 2
    if n == C_MLA - 1 or (C_MLA <= n < C_MLAO and (n - C_MLA) % 2 == 0):
        return 3
    return 1


def slot_count(n):
    return 16 * sum(slot_loads(c) for c in range(n % 2, n + 1, 2))


def build(nc, x, c, ada_w, ada_b, fox_w_in, fox_b_f, fox_w_o, mla_w_a, mla_g_q, mla_g_kv,
          mla_w_uq, mla_w_ukv, mla_w_o, ffn_w_in, ffn_conv_w, ffn_conv_b, ffn_w_out, final_g,
          rope, out):
    with ExitStack() as ctx:
        def sb(name, shape, dt):
            return ctx.enter_context(nc.sbuf_tensor(name, shape, dt))

        def sem(name):
            return ctx.enter_context(nc.semaphore(name))

        xT = sb("xT", [P, DT, S], F32)
        hh = sb("hh", [P, DT, S], F32R)
        hl = sb("hl", [P, DT, S], F32R)
        gh = sb("gh", [P, FFT * S], F32R)
        gl = sb("gl", [P, FFT * S], F32R)
        raw = sb("raw", [P, 2, DT, P], F32)
        wh = sb("wh", [P, 2, DT, P], F32R)
        wl = sb("wl", [P, 2, DT, P], F32R)
        tmp = sb("tmp", [P, 6, S], F32)
        ssq = sb("ssq", [P, S], F32)
        ada_buf = sb("ada_buf", [P, 2, AK, AG], F32)
        ada_acc = sb("ada_acc", [P, 3 * D], F32)
        ada_part = sb("ada_part", [P, AG], F32)
        sel = sb("sel", [P, HEADS, P], BF16)
        cum = sb("cum", [P, S], BF16)
        rope_sb = sb("rope_sb", [P, S], F32)
        ident = sb("ident", [P, P], F32)
        ident_b = sb("ident_b", [P, P], BF16)
        mask_b = sb("mask_b", [P, P], BF16)
        ones = sb("ones", [P, P], F32)
        inv_n = sb("inv_n", [P, 3], F32)
        cols = sb("cols", [P, V_ROWS], F32)
        conv = sb("conv", [P, 2, 4, 2 * FFT], F32)
        mod = sb("mod", [P, SUBS, MODT], F32)
        csil = sb("csil", [P, DT], F32)
        eps = sb("eps", [P, 1], F32)
        bf_sb = sb("bf_sb", [HEADS, 1], F32)
        diag = sb("diag", [P, S], F32)
        stat = sb("stat", [P, 2, QB], F32)
        nmax = sb("nmax", [P, 8], F32)
        rsum = sb("rsum", [P, 8], F32)
        rinv = sb("rinv", [P, 8], F32)

        def bank(name):
            return ctx.enter_context(nc.psum_tensor(name, [P, S], F32))

        PJ = [bank(f"pj{i}") for i in range(2)]
        SC = [bank(f"sc{i}") for i in range(2)]
        TR = [bank(f"tr{i}") for i in range(2)]
        OV = [bank(f"ov{i}") for i in range(2)]

        def tile(g, t):
            return g[:, t * S:(t + 1) * S] if isinstance(t, int) else g[:, bass.ds(t * S, S)]

        PT0 = DT * S

        def pt_off(h, kb, b):
            return PT0 + ((kb * S + b * P) if h == 0 else ((QB - kb) * S + (b - kb) * P))

        def q_tile(g, par):
            return g[:, (13 + 2 * par) * S:(14 + 2 * par) * S]

        def k_tile(g, par):
            return g[:, (14 + 2 * par) * S:(15 + 2 * par) * S]

        def v_all(g):
            return g[:, 17 * S:18 * S]

        def v_half(g, j):
            return v_all(g).rearrange("p (k d) -> p k d", d=P)[:, :, j * HD:(j + 1) * HD]

        def tr_half(bk):
            return TR[bk][:, 0:QB * HD].rearrange("p (k d) -> p k d", d=HD)

        def pt_view(g, h, b):
            o, step = (PT0 + b * P, S) if h == 0 else (PT0 + (QB - b) * S, S + P)
            return g[:, o:o + step * (b + 1)].rearrange("p (k s) -> p k s", s=step)[:, :, 0:P]

        def tr_at(u):
            return u if u == 0 else u + 1

        def pbank(w, par):
            return (T_FOX + 3 * par + w) % 2

        def ccol(l, tap, f):
            return conv[:, l, tap, f:f + 1] if isinstance(f, int) else conv[:, l, tap, bass.ds(f, 1)]

        def rotate(dve, bk, a, b, out_rows, c):
            dve.tensor_tensor(a, bk[HD:MQ, :], rope_sb[HD:MQ, :], ALU.mult).then_inc(rot, 1)
            dve.tensor_tensor(b, bk[MQ:P, :], rope_sb[MQ:P, :], ALU.mult).then_inc(rot, 1)
            dve.wait_ge(rot, c * 2 + 2)
            dve.tensor_tensor(out_rows, a, b, ALU.add).then_inc(rot_ok, 1)

        prob = [tmp[:, i, :] for i in range(2)]
        vT = tmp[:, 2, :]
        rot1, rot2 = tmp[:, 3, :], tmp[:, 4, :]
        fga = [tmp[0:HEADS, i, :] for i in range(6)]
        fgb = tmp[0:HEADS, 3, :].bitcast(BF16)[:, 0:S]
        hpre = [tmp[:, 2 + i, :] for i in range(2)]
        sqb = [tmp[:, i, :] for i in range(2)]

        raw_in = [sem(f"raw_in{i}") for i in range(2)]
        w_hi = sem("w_hi")
        w_lo = sem("w_lo")
        mm = sem("mm")
        ev_a = sem("ev_a")
        ev_d = sem("ev_d")
        vec_in = sem("vec_in")
        conv_in = [sem(f"conv_in{i}") for i in range(2)]
        rest_in = sem("rest_in")
        consts = sem("consts")
        pc = sem("pc")
        cols_t = sem("cols_t")
        cols_r = sem("cols_r")
        x_in = [sem(f"x_in{i}") for i in range(2)]
        x_t = sem("x_t")
        x_e = sem("x_e")
        ada_in = [sem(f"ada_in{i}") for i in range(2)]
        ada_used = sem("ada_used")
        ada_step = sem("ada_step")
        ada_dve = sem("ada_dve")
        ada_cols = sem("ada_cols")
        mod_pre = sem("mod_pre")
        mod_ok = sem("mod_ok")
        sil = sem("sil")
        sq = sem("sq")
        ssq_s = sem("ssq_s")
        mean = sem("mean")
        dev = sem("dev")
        rstd = sem("rstd")
        diag_s = sem("diag_s")
        rb = sem("rb")
        pre = sem("pre")
        h_hi = sem("h_hi")
        h_lo = sem("h_lo")
        cn_pre = sem("cn_pre")
        cn_hi = sem("cn_hi")
        cn_lo = sem("cn_lo")
        fg_d = sem("fg_d")
        fg_a = sem("fg_a")
        cum_ok = sem("cum_ok")
        score = sem("score")
        nmax_s = sem("nmax_s")
        expd = sem("expd")
        rinv_s = sem("rinv_s")
        pn = sem("pn")
        tr_r = sem("tr_r")
        tr_hi = sem("tr_hi")
        tr_lo = sem("tr_lo")
        pv = sem("pv")
        o_hi = sem("o_hi")
        o_lo = sem("o_lo")
        nope = sem("nope")
        rot = sem("rot")
        rot_ok = sem("rot_ok")
        k_hi = sem("k_hi")
        kr_hi = sem("kr_hi")
        kr_lo = sem("kr_lo")
        tap = sem("tap")
        silu_s = sem("silu_s")
        gate_s = sem("gate_s")
        g_hi = sem("g_hi")
        g_lo = sem("g_lo")
        fin = sem("fin")
        fin_t = sem("fin_t")
        fin_e = sem("fin_e")
        out_s = [sem(f"out_s{i}") for i in range(2)]

        xs = [tmp[:, 2 * i:2 * i + 2, :].rearrange("p a s -> p (a s)") for i in range(2)]
        stage = tmp[:, 4:6, :].rearrange("p a (j q) -> p (a j) q", q=P)

        block = ctx.enter_context(nc.Block())

        def landed(n0, i, per):
            return slot_count(n0) if not per else i * (slot_count(n0 + per) - slot_count(n0)) + slot_count(n0)

        @block.sync
        def _(sp):
            vec = stage[:, 0, :]
            for src, r0, n in ((c.rearrange("b (t q) -> (b t) q", q=P), V_C, DT),
                               (ada_b.rearrange("l s (t q) -> (l s t) q", q=P), V_B, SUBS * MODT),
                               (final_g.rearrange("(t q) -> t q", q=P), V_GF, DT),
                               (mla_g_q.rearrange("l (t q) -> (l t) q", q=P), V_GQ, QRT),
                               (mla_g_kv.rearrange("l (t q) -> (l t) q", q=P), V_GKV, KVRT)):
                sp.dma_start(vec[r0:r0 + n, :], src).then_inc(vec_in, 16)
            for t in range(2):
                sp.dma_start(xs[t], x[0, t * P:(t + 1) * P, :]).then_inc(x_in[t], 16)

            def slot_free(n):
                if not isinstance(n, int) or n >= 2:
                    sp.wait_ge(w_hi, n - 1)
                    sp.wait_ge(w_lo, n - 1)

            def load(n0, kt, src, c0=0, c1=P):
                sp.dma_start(raw[:, n0 % 2, 0:kt, c0:c1], src.rearrange("(t p) n -> p t n", p=P)
                             ).then_inc(raw_in[n0 % 2], 16)

            fox = fox_w_in[0]
            load(C_F, DT, fox[:, 3 * D:3 * D + HEADS], 0, HEADS)
            load(C_F, DT, fox[:, 0:P - HEADS], HEADS, P)
            load(C_FOX, DT, fox[:, 0:P])
            sp.dma_start(bf_sb[:, :], fox_b_f.rearrange("l h -> h l")).then_inc(rest_in, 16)
            sp.dma_start(rope_sb[HD:P, :], rope).then_inc(rest_in, 16)
            for l in range(2):
                if l == 1:
                    sp.wait_ge(cols_r, 2)
                for j in range(3):
                    sp.dma_start(stage[0:2 * FFT, 1 + j, :],
                                 ffn_conv_w[l, j].rearrange("(t q) -> t q", q=P)).then_inc(conv_in[l], 16)
                sp.dma_start(stage[0:2 * FFT, 4, :],
                             ffn_conv_b[l].rearrange("(t q) -> t q", q=P)).then_inc(conv_in[l], 16)
            for t in range(2, QB):
                sp.wait_ge(x_t, 2 * (t - 1))
                sp.dma_start(xs[t % 2], x[0, t * P:(t + 1) * P, :]).then_inc(x_in[t % 2], 16)
            for j in range(1, 6):
                slot_free(C_FOX + j)
                load(C_FOX + j, DT, fox[:, (j % 3) * D + (j // 3) * P:(j % 3) * D + (j // 3 + 1) * P])
            with sp.Fori(0, (PAIRS - 2) // 2) as i:
                for j in range(6):
                    slot_free(i * 6 + (C_FOX + 6 + j))
                    load(C_FOX + j, DT, fox[:, bass.ds(i * (2 * P) + ((2 + j // 3) * P + (j % 3) * D), P)])

            def dense(base, src):
                with sp.Fori(0, DT // 2) as i:
                    for j in range(2):
                        slot_free(i * 2 + (base + j))
                        load(base + j, DT, src[:, bass.ds(i * (2 * P) + j * P, P)])

            def mlp(l):
                with sp.Fori(0, FFT) as i:
                    for j in range(2):
                        slot_free(i * 2 + (C_UP[l] + j))
                        load(C_UP[l] + j, DT, ffn_w_in[l][:, bass.ds(i * P + j * FF, P)])
                with sp.Fori(0, DT // 2) as i:
                    for j in range(6):
                        k0 = sum(DOWN_K[:j % 3]) * P
                        kt = DOWN_K[j % 3]
                        slot_free(i * 6 + (C_DOWN[l] + j))
                        load(C_DOWN[l] + j, kt,
                             ffn_w_out[l][k0:k0 + kt * P, bass.ds(i * (2 * P) + (j // 3) * P, P)])

            dense(C_FOXO, fox_w_o[0])
            mlp(0)
            for j in range(QRT + KVRT):
                slot_free(C_MA + j)
                load(C_MA + j, DT, mla_w_a[0][:, j * P:(j + 1) * P])
            r0 = QR + KVR
            slot_free(C_MLA - 1)
            load(C_MLA - 1, DT, mla_w_a[0][:, r0 - HD:r0 + ROPE], 0, MQ)
            load(C_MLA - 1, DT, mla_w_a[0][:, r0 + ROPE // 2:r0 + ROPE], MQ, MQ + ROPE // 2)
            load(C_MLA - 1, DT, mla_w_a[0][:, r0:r0 + ROPE // 2], MQ + ROPE // 2, P)
            with sp.Fori(0, HEADS) as i:
                slot_free(i * 2 + C_MLA)
                uq = mla_w_uq[0]
                load(C_MLA, QRT, uq[:, bass.ds(i * MQ, MQ)], 0, MQ)
                load(C_MLA, QRT, uq[:, bass.ds(i * MQ + (HD + ROPE // 2), ROPE // 2)], MQ, MQ + ROPE // 2)
                load(C_MLA, QRT, uq[:, bass.ds(i * MQ + HD, ROPE // 2)], MQ + ROPE // 2, P)
                slot_free(i * 2 + (C_MLA + 1))
                load(C_MLA + 1, KVRT, mla_w_ukv[0][:, bass.ds(i * P, P)])
            dense(C_MLAO, mla_w_o[0])
            mlp(1)
            for t in range(QB):
                sp.wait_ge(fin_e, 2 * (t + 1))
                sp.dma_start(out[0, t * P:(t + 1) * P, :], xs[t % 2]).then_inc(out_s[t % 2], 16)
            for s in out_s:
                sp.wait_ge(s, 16 * QB // 2)

        @block.gpsimd
        def _(pool):
            pool.memset(ident[:, :], 0.0).then_inc(pc, 1)
            pool.memset(ones[:, :], 1.0).then_inc(consts, 1)
            for j, n in enumerate((D, QR, KVR)):
                pool.memset(inv_n[:, j:j + 1], 1.0 / n).then_inc(consts, 1)
            pool.memset(eps[:, :], EPS).then_inc(consts, 1)
            pool.wait_ge(pc, 1)
            pool.affine_select(out=ident[:, :], in_=ident[:, :], compare_op=ALU.not_equal, fill=1.0,
                               base=0, pattern=[[-1, P]], channel_multiplier=1).then_inc(consts, 1)

            def fetch(k, g, half):
                w = ada_w[k // 2, k % 2][half * AK * P:(half + 1) * AK * P, :]
                src = w[:, bass.ds(g * AG, AG)].rearrange("(t p) n -> p t n", p=P)
                pool.dma_start(ada_buf[:, half, :, :], src).then_inc(ada_in[half], 16)

            for half in range(2):
                fetch(0, 0, half)
            with pool.Fori(1, AGN) as g:
                for half in range(2):
                    pool.wait_ge(ada_used, g * 2 + (half - 1))
                    fetch(0, g, half)

            for t in (ident_b[:, :], mask_b[:, :], sel[:, :, :], cum[:, :]):
                pool.memset(t, 0.0).then_inc(pc, 1)
            pool.wait_ge(pc, 5)
            pool.affine_select(out=ident_b[:, :], in_=ident_b[:, :], compare_op=ALU.not_equal, fill=1.0,
                               base=0, pattern=[[-1, P]], channel_multiplier=1).then_inc(pc, 1)
            pool.affine_select(out=mask_b[:, :], in_=mask_b[:, :], compare_op=ALU.is_ge, fill=MASKED,
                               base=0, pattern=[[-1, P]], channel_multiplier=1).then_inc(pc, 1)
            for part in range(3):
                pool.wait_ge(pc, 7 + part)
                pool.affine_select(out=sel[:, :, :], in_=sel[:, :, :], compare_op=ALU.not_equal, fill=1.0,
                                   base=-32 * part, pattern=[[-1, HEADS], [0, P]], channel_multiplier=1
                                   ).then_inc(pc, 1)

            def group(k, g, last):
                for half in range(2):
                    buf = ada_buf[:, half, :, :]
                    used = g * 2 + (AH * k + half)
                    s0 = g * 5 + (5 * AGN * (k - 1) + 2 * half)
                    pool.wait_ge(ada_in[half], g * 16 + 16 * (AGN * k + 1))
                    coef = csil[:, half * AK:(half + 1) * AK].rearrange("p (t o) -> p t o", o=1)
                    pool.tensor_tensor(buf, buf, coef.to_broadcast([P, AK, AG]), ALU.mult).then_inc(ada_step, 1)
                    pool.wait_ge(ada_step, s0 + 1)
                    pool.tensor_tensor(buf[:, 0:2, :], buf[:, 0:2, :], buf[:, 2:4, :], ALU.add
                                       ).then_inc(ada_step, 1)
                    pool.wait_ge(ada_step, s0 + 2)
                    if half == 0:
                        pool.tensor_tensor(ada_part[:, :], buf[:, 0, :], buf[:, 1, :], ALU.add).then_inc(ada_used, 1)
                    else:
                        pool.tensor_tensor(buf[:, 0, :], buf[:, 0, :], buf[:, 1, :], ALU.add
                                           ).then_inc(ada_step, 1)
                        pool.wait_ge(ada_step, s0 + 3)
                        pool.wait_ge(ada_used, used)
                        pool.tensor_tensor(ada_acc[:, bass.ds(g * AG, AG)], ada_part[:, :], buf[:, 0, :],
                                           ALU.add).then_inc(ada_used, 1)
                    if not last:
                        pool.wait_ge(ada_used, used + 1)
                        fetch(k, g + 1, half)

            pool.wait_ge(sil, 1)
            for k in range(1, SUBS):
                pool.wait_ge(ada_cols, k)
                for half in range(2):
                    fetch(k, 0, half)
                with pool.Fori(0, AGN - 1) as g:
                    group(k, g, False)
                group(k, AGN - 1, True)

        @block.scalar
        def _(act):
            def split(n0, i=0, per=0):
                kt = chunk_k(n0)
                n = i * per + n0
                act.wait_ge(raw_in[n0 % 2], landed(n0, i, per))
                if per or n0 >= 2:
                    act.wait_ge(mm, n - 1)
                act.activation(wh[:, n0 % 2, 0:kt, :], raw[:, n0 % 2, 0:kt, :], ACT.Copy).then_inc(w_hi, 1)

            def norm(n):
                act.wait_ge(mean, n + 1)
                act.activation(stat[:, 0, :], OV[0][:, 0:QB], ACT.Sqrt, bias=eps[:, 0:1]).then_inc(dev, 1)

            def modulated(k):
                act.wait_ge(mod_ok, k + 1)
                for kt in range(DT):
                    act.wait_ge(pre, DT * k + kt + 1)
                    act.activation(hh[:, kt, :], hpre[kt % 2], ACT.Identity,
                                   bias=mod[:, k, kt:kt + 1]).then_inc(h_hi, 1)

            act.wait_ge(cols_t, 1)
            act.activation(cols[:, :], TR[0][:, 0:V_ROWS], ACT.Copy).then_inc(cols_r, 1)
            act.wait_ge(cols_r, 1)
            act.activation(csil[:, :], cols[:, V_C:V_C + DT], ACT.Silu).then_inc(sil, 1)
            split(0)
            split(1)
            for l in range(2):
                act.wait_ge(cols_t, l + 2)
                act.activation(conv[:, l, :, :], TR[(l + 1) % 2][:, 0:8 * FFT], ACT.Copy).then_inc(cols_r, 1)
            for t in range(QB):
                for f in range(2):
                    act.wait_ge(x_t, 2 * t + f + 1)
                    act.activation(xT[:, 4 * f:4 * f + 4, t * P:(t + 1) * P], SC[f][:, :], ACT.Copy
                                   ).then_inc(x_e, 1)
            act.wait_ge(x_e, 2 * QB)
            for kt in range(DT):
                if kt >= 2:
                    act.wait_ge(ssq_s, kt)
                act.activation(sqb[kt % 2], xT[:, kt, :], ACT.Square).then_inc(sq, 1)
            norm(0)
            modulated(0)
            split(2)
            act.wait_ge(ev_d, T_F + 1)
            act.activation(fga[2], fga[0], ACT.Abs).then_inc(ev_a, 1)
            act.wait_ge(ev_a, T_F + 1)
            act.activation(fga[3], fga[2], ACT.Exp, scale=-1.0).then_inc(fg_a, 1)
            act.wait_ge(fg_a, 1)
            act.activation(fga[4], fga[3], ACT.Ln, bias=ones[0:HEADS, 0:1]).then_inc(fg_a, 1)

            def fox_q(n, par):
                act.wait_ge(mm, n + 1)
                act.activation(q_tile(gh, par), PJ[pbank(0, par)][:, :], ACT.Copy, scale=FOX_SCALE
                               ).then_inc(ev_a, 1)

            def fox_k(n, par):
                act.wait_ge(mm, n + 1)
                act.activation(k_tile(gh, par), PJ[pbank(1, par)][:, :], ACT.Copy).then_inc(ev_a, 1)

            def fox_v(n, par):
                act.wait_ge(mm, n + 1)
                act.activation(vT[:, 0:S // 2], PJ[pbank(2, par)][:, 0:S // 2], ACT.Copy).then_inc(ev_a, 1)

            for j, take in enumerate((fox_q, fox_k, fox_v)):
                act.wait_ge(mm, C_FOX + j + 1)
                split(C_FOX + j + 2)
                take(C_FOX + j, 0)

            def exp(u, unit):
                nc_ = (u % QB + 1) * P
                act.wait_ge(nmax_s, unit + 1)
                act.activation(prob[u % 2][:, 0:nc_], SC[u % 2][:, 0:nc_], ACT.Exp,
                               bias=nmax[:, u:u + 1], accum_out=rsum[:, u:u + 1]).then_inc(expd, 1)

            def turned(h, b, r, bk):
                act.wait_ge(tr_r, r + 1)
                act.activation(pt_view(gh, h, b), TR[bk][:, 0:(b + 1) * P].rearrange("p (k q) -> p k q", q=P),
                               ACT.Copy).then_inc(tr_hi, 1)

            def o_take(h, t, hd):
                act.wait_ge(pv, hd + 1)
                rows = slice(h * HD, (h + 1) * HD)
                act.activation(tile(gh, t)[rows, :], OV[h][rows, :], ACT.Copy).then_inc(o_hi, 1)

            def fox_pair(i, j, proj, nxt):
                par = j
                t = i * 2 + j
                U = i * (4 * QB) + (U_FOX + 2 * QB * j)
                R = i * (2 * FOX_TR) + (R_FOX + FOX_TR * j)
                n0 = C_FOX + 3 * (j + 1)
                for u in range(2 * QB):
                    exp(u, U + u)
                    if u >= 1:
                        turned((u - 1) // QB, (u - 1) % QB, R + tr_at(u - 1), (FOX_TR * j + tr_at(u - 1)) % 2)
                    if u == 1:
                        act.wait_ge(tr_r, R + 2)
                        act.activation(v_all(gh), TR[(FOX_TR * j + 1) % 2][:, :], ACT.Copy).then_inc(tr_hi, 1)
                    if proj and u == 4:
                        split_after(n0, i, 6, nxt)
                        fox_q(i * 6 + n0, 1 - par)
                    if u == 6:
                        o_take(0, t, i * 4 + (H_FOX + 2 * j))
                    if proj and u == 7:
                        split_after(n0 + 1, i, 6, nxt)
                        fox_k(i * 6 + (n0 + 1), 1 - par)
                turned(1, QB - 1, R + tr_at(7), (FOX_TR * j + tr_at(7)) % 2)
                if proj:
                    split_after(n0 + 2, i, 6, nxt)
                    fox_v(i * 6 + (n0 + 2), 1 - par)
                o_take(1, t, i * 4 + (H_FOX + 2 * j + 1))

            def split_after(n0, i, per, nxt):
                act.wait_ge(mm, i * per + (n0 + 1))
                if nxt is None:
                    split(n0 + 2, i, per)
                else:
                    split(nxt + n0 + 2)

            with act.Fori(0, PAIRS // 2 - 1) as i:
                for j in range(2):
                    fox_pair(i, j, True, None)
            last = PAIRS // 2 - 1
            fox_pair(last, 0, True, 6 * last)
            fox_pair(last, 1, False, None)

            def residual(m, tile0, norm_n, j):
                act.wait_ge(ev_d, tile0 + 1)
                act.wait_ge(ssq_s, m + SSQ_END[norm_n - 1])
                src = xT[:, m, :] if isinstance(m, int) else xT[:, bass.ds(m, 1), :]
                act.activation(sqb[j % 2], src, ACT.Square).then_inc(ev_a, 1)

            def dense(C, T, norm_n):
                def step(i, j, nxt):
                    split_after(C + j, i, 2, nxt)
                    residual(i * 2 + j, i * 2 + (T + j), norm_n, j)
                with act.Fori(0, DT // 2 - 1) as i:
                    for j in range(2):
                        step(i, j, None)
                for j in range(2):
                    step(DT // 2 - 1, j, DT - 2)

            def mlp(l, norm_n):
                C, T = C_UP[l], T_UP[l]

                def pair(i, par, nxt):
                    m = i * 2 + par
                    for side, y in ((0, tmp[:, par, :]), (1, tmp[:, 2 + par, :])):
                        j = 2 * par + side
                        split_after(C + j, i, 4, nxt)
                        f = m + side * FFT
                        act.activation(y, PJ[(T + j) % 2][:, :], ACT.Identity, bias=ccol(l, 3, f),
                                       scale=ccol(l, 2, f)).then_inc(ev_a, 1)
                    act.wait_ge(ev_d, i * 4 + (T + 2 * par + 1))
                    act.activation(tmp[:, par, :], tmp[:, par, :], ACT.Silu).then_inc(silu_s, 1)
                    act.wait_ge(gate_s, m + (FFT * l + 1))
                    act.activation(tile(gh, m), tmp[:, 2 + par, :], ACT.Copy).then_inc(g_hi, 1)

                with act.Fori(0, FFT // 2 - 1) as i:
                    for par in range(2):
                        pair(i, par, None)
                for par in range(2):
                    pair(FFT // 2 - 1, par, 4 * (FFT // 2 - 1))

                C, T = C_DOWN[l], T_DOWN[l]

                def down(i, nxt):
                    for j in range(6):
                        if nxt is not None and C + nxt + j + 2 >= C_END:
                            act.wait_ge(mm, C + nxt + j + 1)
                        else:
                            split_after(C + j, i, 6, nxt)
                        if j % 3 == 2:
                            residual(i * 2 + j // 3, i * 2 + (T + j // 3), norm_n, j // 3)
                with act.Fori(0, DT // 2 - 1) as i:
                    down(i, None)
                down(DT // 2 - 1, 6 * (DT // 2 - 1))

            dense(C_FOXO, T_FOXO, 1)
            norm(1)
            modulated(1)
            mlp(0, 2)
            norm(2)
            modulated(2)
            for j in range(QRT + KVRT + 1):
                act.wait_ge(mm, C_MA + j + 1)
                split(C_MA + j + 2)
                if j < QRT + KVRT:
                    done = SSQ_END[N_CQ - 1] + 1 + j + (1 if j >= QRT else 0)
                    if j > 0:
                        act.wait_ge(ssq_s, done - (1 if j == QRT else 0))
                    act.activation(tmp[:, 5, :], PJ[(T_MA + j) % 2][:, :], ACT.Square).then_inc(ev_a, 1)
                    if j == QRT:
                        norm(N_CQ)
                else:
                    act.wait_ge(rot_ok, 1)
                    for par in range(2):
                        act.activation(k_tile(gh, par)[HD:MQ, :], tmp[HD:MQ, 5, :], ACT.Copy
                                       ).then_inc(ev_a if par else kr_hi, 1)
            norm(N_CKV)
            for j in range(QRT + KVRT):
                act.wait_ge(cn_pre, j + 1)
                act.activation(hh[:, j, :], tmp[:, j, :], ACT.Copy).then_inc(cn_hi, 1)

            def mla_take(h, par, n_q, first):
                act.wait_ge(mm, n_q + 1)
                act.activation(rot1[0:HD, :], PJ[T_MLA % 2][0:HD, :], ACT.Copy).then_inc(nope, 1)
                act.wait_ge(nope, h + 1)
                act.wait_ge(rot_ok, h + 2)
                act.activation(q_tile(gh, par)[0:MQ, :], rot1[0:MQ, :], ACT.Copy, scale=MLA_SCALE
                               ).then_inc(ev_a, 1)

            def mla_take_kv(par, n_kv):
                act.wait_ge(mm, n_kv + 1)
                act.activation(k_tile(gh, par)[0:HD, :], PJ[(T_MLA + 1) % 2][0:HD, :], ACT.Copy).then_inc(k_hi, 1)
                act.activation(vT[0:HD, :], PJ[(T_MLA + 1) % 2][HD:P, :], ACT.Copy).then_inc(ev_a, 1)

            split_after(C_MLA, 0, 0, 0)
            mla_take(0, 0, C_MLA, True)
            split_after(C_MLA + 1, 0, 0, 0)
            mla_take_kv(0, C_MLA + 1)

            def mla_head(t, j, proj, nxt):
                hd = t * 2 + j
                U = t * (2 * QB) + (U_MLA + QB * j)
                R = t * (2 * MLA_TR) + (R_MLA + MLA_TR * j)
                n0 = C_MLA + 2 * (j + 1)
                for b in range(QB):
                    exp(QB * j + b, U + b)
                    if b >= 1:
                        turned(j, b - 1, R + tr_at(b - 1), (R_MLA + MLA_TR * j + tr_at(b - 1)) % 2)
                    if b == 1:
                        act.wait_ge(tr_r, R + 2)
                        act.activation(v_half(gh, j), tr_half((R_MLA + MLA_TR * j + 1) % 2), ACT.Copy
                                       ).then_inc(tr_hi, 1)
                    if proj and b == 3:
                        split_after(n0, t, 4, nxt)
                        mla_take(hd + 1, 1 - j, t * 4 + n0, False)
                turned(j, QB - 1, R + tr_at(QB - 1), (R_MLA + MLA_TR * j + tr_at(QB - 1)) % 2)
                if proj:
                    split_after(n0 + 1, t, 4, nxt)
                    mla_take_kv(1 - j, t * 4 + (n0 + 1))
                o_take(j, t, t * 2 + (H_MLA + j))

            with act.Fori(0, HEADS // 2 - 1) as t:
                for j in range(2):
                    mla_head(t, j, True, None)
            last = HEADS // 2 - 1
            mla_head(last, 0, True, 4 * last)
            mla_head(last, 1, False, None)
            dense(C_MLAO, T_MLAO, 5)
            norm(5)
            modulated(3)
            mlp(1, 6)
            norm(6)
            for t in range(QB):
                for f in range(2):
                    act.wait_ge(fin_t, 2 * t + f + 1)
                    if t >= 2:
                        act.wait_ge(out_s[t % 2], 16 * (t // 2))
                    act.activation(xs[t % 2][:, f * S:(f + 1) * S], SC[f][:, :], ACT.Copy).then_inc(fin_e, 1)

        @block.vector
        def _(dve):
            def f32(ap):
                return ap.bitcast(F32)

            def split(n0, i=0, per=0):
                kt = chunk_k(n0)
                dve.wait_ge(w_hi, i * per + (n0 + 1))
                dve.tensor_tensor(wl[:, n0 % 2, 0:kt, :], raw[:, n0 % 2, 0:kt, :],
                                  f32(wh[:, n0 % 2, 0:kt, :]), ALU.subtract).then_inc(w_lo, 1)

            def split_after(n0, i, per, nxt):
                if nxt is None:
                    split(n0 + 2, i, per)
                elif nxt + n0 + 2 < C_END:
                    split(nxt + n0 + 2)

            def modulation(k):
                dve.wait_ge(ada_cols, k + 1)
                dve.tensor_tensor(mod[:, k, :], OV[1][:, 0:MODT],
                                  cols[:, V_B + MODT * k:V_B + MODT * (k + 1)], ALU.add).then_inc(mod_pre, 1)
                dve.wait_ge(mod_pre, k + 1)
                dve.tensor_scalar(mod[:, k, DT:2 * DT], mod[:, k, DT:2 * DT], 1.0, None, ALU.add
                                  ).then_inc(mod_ok, 1)

            def norm(n):
                dve.wait_ge(dev, n + 1)
                if n:
                    dve.wait_ge(diag_s, n)
                dve.reciprocal(stat[:, 1, :], stat[:, 0, :]).then_inc(rstd, 1)
                dve.wait_ge(rstd, n + 1)
                for b in range(QB):
                    ins = dve.tensor_scalar(diag[:, b * P:(b + 1) * P], ident[:, :], stat[:, 1, b:b + 1],
                                            None, ALU.mult)
                ins.then_inc(diag_s, 1)

            def modulated(k, norm_n):
                dve.wait_ge(mod_ok, k + 1)
                dve.wait_ge(rb, norm_n + 1)

                def low(kt):
                    dve.wait_ge(h_hi, DT * k + kt + 1)
                    dve.scalar_tensor_tensor(out=hl[:, kt, :], in0=hpre[kt % 2], scalar=mod[:, k, kt:kt + 1],
                                             in1=f32(hh[:, kt, :]), op0=ALU.add, op1=ALU.subtract
                                             ).then_inc(h_lo, 1)
                for kt in range(DT):
                    if kt >= 2:
                        dve.wait_ge(h_lo, DT * k + kt - 1)
                    dve.scalar_tensor_tensor(out=hpre[kt % 2], in0=xT[:, kt, :],
                                             scalar=mod[:, k, DT + kt:DT + kt + 1], in1=OV[1][:, :],
                                             op0=ALU.mult, op1=ALU.mult).then_inc(pre, 1)
                    if kt:
                        low(kt - 1)
                low(DT - 1)

            dve.wait_ge(sil, 1)
            with dve.Fori(0, AGN) as g:
                acc = ada_acc[:, bass.ds(g * AG, AG)]
                for half in range(2):
                    dve.wait_ge(ada_in[half], g * 16 + 16)
                    for t in range(AK):
                        kt = half * AK + t
                        w = ada_buf[:, half, t, :]
                        if kt == 0:
                            dve.tensor_scalar(acc, w, csil[:, 0:1], None, ALU.mult).then_inc(ada_dve, 1)
                            continue
                        dve.wait_ge(ada_dve, g * (DT - 2) + (kt - (1 if kt > AK - 1 else 0)))
                        if kt == AK:
                            dve.wait_ge(ada_used, g * 2 + 1)
                        ins = dve.scalar_tensor_tensor(out=acc, in0=w, scalar=csil[:, kt:kt + 1], in1=acc,
                                                       op0=ALU.mult, op1=ALU.add)
                        ins.then_inc(ada_used if t == AK - 1 else ada_dve, 1)
            dve.memset(ssq[:, :], 0.0).then_inc(ssq_s, 1)
            for kt in range(DT):
                dve.wait_ge(sq, kt + 1)
                dve.wait_ge(ssq_s, kt + 1)
                dve.tensor_tensor(ssq[:, :], ssq[:, :], sqb[kt % 2], ALU.add).then_inc(ssq_s, 1)
            split(0)
            split(1)
            modulation(0)
            norm(0)
            modulated(0, 0)
            split(2)
            dve.memset(fga[5], 1.0).then_inc(fg_d, 1)
            dve.wait_ge(mm, C_F + 1)
            dve.wait_ge(rest_in, 32)
            dve.tensor_scalar(fga[0], PJ[T_F % 2][0:HEADS, :], bf_sb[:, 0:1], None, ALU.add).then_inc(ev_d, 1)
            dve.wait_ge(ev_d, T_F + 1)
            dve.tensor_scalar(fga[1], fga[0], 0.0, None, ALU.min).then_inc(fg_d, 1)
            dve.wait_ge(fg_d, 2)
            dve.wait_ge(fg_a, 2)
            dve.tensor_tensor(fga[4], fga[4], fga[1], ALU.subtract).then_inc(fg_d, 1)
            dve.wait_ge(fg_d, 3)
            dve.tensor_tensor_scan(fga[0], fga[5], fga[4], 0.0, ALU.mult, ALU.add).then_inc(fg_d, 1)
            dve.wait_ge(fg_d, 4)
            dve.wait_ge(pc, 10)
            dve.tensor_copy(cum[0:HEADS, :], fga[0]).then_inc(fg_d, 1)
            dve.wait_ge(fg_d, 5)
            dve.tensor_tensor(fga[1], fga[0], cum[0:HEADS, :], ALU.subtract).then_inc(fg_d, 1)
            dve.wait_ge(fg_d, 6)
            dve.tensor_copy(fgb, fga[1]).then_inc(fg_d, 1)
            dve.wait_ge(fg_d, 7)
            dve.tensor_copy(cum[32:32 + HEADS, :], fgb).then_inc(cum_ok, 1)
            dve.tensor_tensor(fga[4], fga[1], fgb, ALU.subtract).then_inc(fg_d, 1)
            dve.wait_ge(fg_d, 8)
            dve.tensor_copy(cum[64:64 + HEADS, :], fga[4]).then_inc(cum_ok, 1)

            def fox_q(n_tile, par):
                dve.wait_ge(ev_a, n_tile + 1)
                dve.scalar_tensor_tensor(out=q_tile(gl, par), in0=PJ[pbank(0, par)][:, :], scalar=FOX_SCALE,
                                         in1=f32(q_tile(gh, par)), op0=ALU.mult, op1=ALU.subtract
                                         ).then_inc(ev_d, 1)

            def fox_k(n_tile, par):
                dve.wait_ge(ev_a, n_tile + 1)
                dve.tensor_tensor(k_tile(gl, par), PJ[pbank(1, par)][:, :], f32(k_tile(gh, par)), ALU.subtract
                                  ).then_inc(ev_d, 1)

            def fox_v(n_tile, par):
                dve.wait_ge(ev_a, n_tile + 1)
                dve.tensor_copy(vT[:, S // 2:S], PJ[pbank(2, par)][:, S // 2:S]).then_inc(ev_d, 1)

            for j, take in enumerate((fox_q, fox_k, fox_v)):
                split(C_FOX + j + 2)
                take(T_FOX + j, 0)

            def maximum(u, unit):
                nc_ = (u % QB + 1) * P
                dve.wait_ge(score, unit + 1)
                dve.tensor_reduce(nmax[:, u:u + 1], SC[u % 2][:, 0:nc_], AX.X, ALU.max, negate=True
                                  ).then_inc(nmax_s, 1)

            def normalise(u, unit):
                nc_ = (u % QB + 1) * P
                dve.wait_ge(expd, unit + 1)
                dve.reciprocal(rinv[:, u:u + 1], rsum[:, u:u + 1]).then_inc(rinv_s, 1)
                dve.wait_ge(rinv_s, unit + 1)
                dve.tensor_scalar(prob[u % 2][:, 0:nc_], prob[u % 2][:, 0:nc_], rinv[:, u:u + 1], None,
                                  ALU.mult).then_inc(pn, 1)

            def turned(h, b, r, bk):
                dve.wait_ge(tr_hi, r + 1)
                dve.tensor_tensor(pt_view(gl, h, b), TR[bk][:, 0:(b + 1) * P].rearrange("p (k q) -> p k q", q=P),
                                  f32(pt_view(gh, h, b)), ALU.subtract).then_inc(tr_lo, 1)

            def o_take(h, t, hd):
                dve.wait_ge(o_hi, hd + 1)
                rows = slice(h * HD, (h + 1) * HD)
                dve.tensor_tensor(tile(gl, t)[rows, :], OV[h][rows, :], f32(tile(gh, t)[rows, :]), ALU.subtract
                                  ).then_inc(o_lo, 1)

            def fox_pair(i, j, proj, nxt):
                par = j
                t = i * 2 + j
                U = i * (4 * QB) + (U_FOX + 2 * QB * j)
                R = i * (2 * FOX_TR) + (R_FOX + FOX_TR * j)
                n0 = C_FOX + 3 * (j + 1)
                t0 = i * 6 + (T_FOX + 3 * (j + 1))
                for u in range(2 * QB + 1):
                    if u < 2 * QB:
                        maximum(u, U + u)
                    if u >= 1:
                        normalise(u - 1, U + (u - 1))
                    if u >= 2:
                        turned((u - 2) // QB, (u - 2) % QB, R + tr_at(u - 2), (FOX_TR * j + tr_at(u - 2)) % 2)
                    if u == 2:
                        dve.wait_ge(tr_hi, R + 2)
                        dve.tensor_tensor(v_all(gl), TR[(FOX_TR * j + 1) % 2][:, :], f32(v_all(gh)),
                                          ALU.subtract).then_inc(tr_lo, 1)
                    if proj and u == 5:
                        split_after(n0, i, 6, nxt)
                        fox_q(t0, 1 - par)
                    if u == 7:
                        o_take(0, t, i * 4 + (H_FOX + 2 * j))
                    if proj and u == 8:
                        split_after(n0 + 1, i, 6, nxt)
                        fox_k(t0 + 1, 1 - par)
                turned(1, QB - 1, R + tr_at(7), (FOX_TR * j + tr_at(7)) % 2)
                if proj:
                    split_after(n0 + 2, i, 6, nxt)
                    fox_v(t0 + 2, 1 - par)
                o_take(1, t, i * 4 + (H_FOX + 2 * j + 1))

            with dve.Fori(0, PAIRS // 2 - 1) as i:
                for j in range(2):
                    fox_pair(i, j, True, None)
            last = PAIRS // 2 - 1
            fox_pair(last, 0, True, 6 * last)
            fox_pair(last, 1, False, None)

            def xtile(m):
                return xT[:, m, :] if isinstance(m, int) else xT[:, bass.ds(m, 1), :]

            def residual(m, j, tile_n, bk, k, norm_n):
                g = mod[:, k, 2 * DT + m:2 * DT + m + 1] if isinstance(m, int) else \
                    mod[:, k, bass.ds(m + 2 * DT, 1)]
                dve.scalar_tensor_tensor(out=xtile(m), in0=PJ[bk][:, :], scalar=g, in1=xtile(m),
                                         op0=ALU.mult, op1=ALU.add).then_inc(ev_d, 1)
                dve.wait_ge(ev_a, tile_n + 1)
                dve.wait_ge(ssq_s, m + (SSQ_END[norm_n - 1] + 1))
                dve.tensor_tensor(ssq[:, :], ssq[:, :], sqb[j % 2], ALU.add).then_inc(ssq_s, 1)

            def dense(C, T, k, norm_n):
                def step(i, j, nxt):
                    split_after(C + j, i, 2, nxt)
                    dve.wait_ge(mm, i * 2 + (C + j + 1))
                    residual(i * 2 + j, j, i * 2 + (T + j), (T + j) % 2, k, norm_n)
                dve.memset(ssq[:, :], 0.0).then_inc(ssq_s, 1)
                with dve.Fori(0, DT // 2 - 1) as i:
                    for j in range(2):
                        step(i, j, None)
                for j in range(2):
                    step(DT // 2 - 1, j, DT - 2)

            def mlp(l, k, norm_n):
                C, T = C_UP[l], T_UP[l]

                def pair(i, par, nxt):
                    m = i * 2 + par
                    yg, yv = tmp[:, par, :], tmp[:, 2 + par, :]
                    for side, y in ((0, yg), (1, yv)):
                        j = 2 * par + side
                        bk = PJ[(T + j) % 2]
                        f = m + side * FFT
                        split_after(C + j, i, 4, nxt)
                        dve.wait_ge(ev_a, i * 4 + (T + j + 1))
                        dve.scalar_tensor_tensor(out=y[:, 1:S], in0=bk[:, 0:S - 1], scalar=ccol(l, 1, f),
                                                 in1=y[:, 1:S], op0=ALU.mult, op1=ALU.add).then_inc(tap, 1)
                        dve.wait_ge(tap, i * 4 + (2 * FFT * l + j + 1))
                        dve.scalar_tensor_tensor(out=y[:, 2:S], in0=bk[:, 0:S - 2], scalar=ccol(l, 0, f),
                                                 in1=y[:, 2:S], op0=ALU.mult, op1=ALU.add).then_inc(ev_d, 1)
                    dve.wait_ge(silu_s, m + (FFT * l + 1))
                    dve.wait_ge(ev_d, i * 4 + (T + 2 * par + 2))
                    dve.tensor_tensor(yv, yg, yv, ALU.mult).then_inc(gate_s, 1)
                    dve.wait_ge(g_hi, m + (FFT * l + 1))
                    dve.tensor_tensor(tile(gl, m), yv, f32(tile(gh, m)), ALU.subtract).then_inc(g_lo, 1)

                with dve.Fori(0, FFT // 2 - 1) as i:
                    for par in range(2):
                        pair(i, par, None)
                for par in range(2):
                    pair(FFT // 2 - 1, par, 4 * (FFT // 2 - 1))

                C, T = C_DOWN[l], T_DOWN[l]

                def down(i, nxt):
                    for j in range(6):
                        split_after(C + j, i, 6, nxt)
                        if j % 3 == 2:
                            dve.wait_ge(mm, i * 6 + (C + j + 1))
                            residual(i * 2 + j // 3, j // 3, i * 2 + (T + j // 3), (T + j // 3) % 2, k, norm_n)
                dve.memset(ssq[:, :], 0.0).then_inc(ssq_s, 1)
                with dve.Fori(0, DT // 2 - 1) as i:
                    down(i, None)
                down(DT // 2 - 1, 6 * (DT // 2 - 1))

            dense(C_FOXO, T_FOXO, 0, 1)
            modulation(1)
            norm(1)
            modulated(1, 1)
            mlp(0, 1, 2)
            modulation(2)
            norm(2)
            modulated(2, 2)
            s0 = SSQ_END[N_CQ - 1]
            dve.memset(ssq[:, :], 0.0).then_inc(ssq_s, 1)
            for j in range(QRT + KVRT + 1):
                bk = PJ[(T_MA + j) % 2]
                split(C_MA + j + 2)
                dve.wait_ge(ev_a, T_MA + j + 1) if j < QRT + KVRT else dve.wait_ge(mm, C_MA + j + 1)
                if j < QRT + KVRT:
                    dve.tensor_copy(tmp[:, j, :], bk[:, :]).then_inc(ev_d, 1)
                    extra = 1
                    if j == QRT:
                        dve.wait_ge(mean, N_CQ + 1)
                        dve.memset(ssq[:, :], 0.0).then_inc(ssq_s, 1)
                    if j >= QRT:
                        extra = 2
                    dve.wait_ge(ssq_s, s0 + j + extra)
                    dve.tensor_tensor(ssq[:, :], ssq[:, :], tmp[:, 5, :], ALU.add).then_inc(ssq_s, 1)
                    if j == QRT:
                        norm(N_CQ)
                else:
                    dve.wait_ge(ssq_s, SSQ_END[N_CKV])
                    rotate(dve, bk, tmp[0:ROPE, 5, :], rope_sb[0:ROPE, :], tmp[HD:MQ, 5, :], 0)
                    dve.wait_ge(kr_hi, 1)
                    dve.tensor_tensor(k_tile(gl, 0)[HD:MQ, :], tmp[HD:MQ, 5, :],
                                      f32(k_tile(gh, 0)[HD:MQ, :]), ALU.subtract).then_inc(kr_lo, 1)
                    dve.wait_ge(ev_a, T_MA + j + 1)
                    dve.tensor_tensor(k_tile(gl, 1)[HD:MQ, :], tmp[HD:MQ, 5, :],
                                      f32(k_tile(gh, 1)[HD:MQ, :]), ALU.subtract).then_inc(ev_d, 1)

            def latent(j, n, gcol):
                dve.wait_ge(rb, n + 1)
                dve.scalar_tensor_tensor(out=tmp[:, j, :], in0=tmp[:, j, :], scalar=cols[:, gcol:gcol + 1],
                                         in1=OV[1][:, :], op0=ALU.mult, op1=ALU.mult).then_inc(cn_pre, 1)

            dve.wait_ge(ev_d, T_MA + QRT + KVRT)
            for j in range(QRT):
                latent(j, N_CQ, V_GQ + j)
            norm(N_CKV)
            for j in range(KVRT):
                latent(QRT + j, N_CKV, V_GKV + j)
            for j in range(QRT + KVRT):
                dve.wait_ge(cn_hi, j + 1)
                dve.tensor_tensor(hl[:, j, :], tmp[:, j, :], f32(hh[:, j, :]), ALU.subtract).then_inc(cn_lo, 1)

            def mla_take(h, par, n_q, tile_q):
                dve.wait_ge(mm, n_q + 1)
                rotate(dve, PJ[T_MLA % 2], rot1[HD:MQ, :], rot2[HD:MQ, :], rot1[HD:MQ, :], h + 1)
                dve.wait_ge(ev_a, tile_q + 1)
                dve.scalar_tensor_tensor(out=q_tile(gl, par)[0:MQ, :], in0=rot1[0:MQ, :], scalar=MLA_SCALE,
                                         in1=f32(q_tile(gh, par)[0:MQ, :]), op0=ALU.mult, op1=ALU.subtract
                                         ).then_inc(ev_d, 1)

            def mla_take_kv(h, par, tile_kv):
                dve.wait_ge(ev_a, tile_kv + 1)
                dve.wait_ge(k_hi, h + 1)
                dve.tensor_tensor(k_tile(gl, par)[0:HD, :], PJ[(T_MLA + 1) % 2][0:HD, :],
                                  f32(k_tile(gh, par)[0:HD, :]), ALU.subtract).then_inc(ev_d, 1)

            split_after(C_MLA, 0, 0, 0)
            mla_take(0, 0, C_MLA, T_MLA)
            split_after(C_MLA + 1, 0, 0, 0)
            mla_take_kv(0, 0, T_MLA + 1)

            def mla_head(t, j, proj, nxt):
                hd = t * 2 + j
                U = t * (2 * QB) + (U_MLA + QB * j)
                R = t * (2 * MLA_TR) + (R_MLA + MLA_TR * j)
                n0 = C_MLA + 2 * (j + 1)
                t0 = t * 4 + (T_MLA + 2 * (j + 1))
                for b in range(QB + 1):
                    if b < QB:
                        maximum(QB * j + b, U + b)
                    if b >= 1:
                        normalise(QB * j + b - 1, U + (b - 1))
                    if b >= 2:
                        turned(j, b - 2, R + tr_at(b - 2), (R_MLA + MLA_TR * j + tr_at(b - 2)) % 2)
                    if b == 2:
                        dve.wait_ge(tr_hi, R + 2)
                        dve.tensor_tensor(v_half(gl, j), tr_half((R_MLA + MLA_TR * j + 1) % 2),
                                          f32(v_half(gh, j)), ALU.subtract).then_inc(tr_lo, 1)
                    if proj and b == 4:
                        split_after(n0, t, 4, nxt)
                        mla_take(hd + 1, 1 - j, t * 4 + n0, t0)
                turned(j, QB - 1, R + tr_at(QB - 1), (R_MLA + MLA_TR * j + tr_at(QB - 1)) % 2)
                if proj:
                    split_after(n0 + 1, t, 4, nxt)
                    mla_take_kv(hd + 1, 1 - j, t0 + 1)
                o_take(j, t, t * 2 + (H_MLA + j))

            with dve.Fori(0, HEADS // 2 - 1) as t:
                for j in range(2):
                    mla_head(t, j, True, None)
            last = HEADS // 2 - 1
            mla_head(last, 0, True, 4 * last)
            mla_head(last, 1, False, None)
            dense(C_MLAO, T_MLAO, 2, 5)
            modulation(3)
            norm(5)
            modulated(3, 5)
            mlp(1, 3, 6)
            norm(6)
            dve.wait_ge(rb, N_FINAL + 1)
            for kt in range(DT):
                dve.scalar_tensor_tensor(out=xT[:, kt, :], in0=xT[:, kt, :],
                                         scalar=cols[:, V_GF + kt:V_GF + kt + 1], in1=OV[1][:, :],
                                         op0=ALU.mult, op1=ALU.mult).then_inc(fin, 1)

        @block.tensor
        def _(pe):
            def product(n0, i, per, j0, j1, rh, rl, bank_, start=True, stop=True):
                s = n0 % 2
                kts = chunk_k(n0)
                if j0 == 0:
                    pe.wait_ge(w_hi, i * per + (n0 + 1))
                    pe.wait_ge(w_lo, i * per + (n0 + 1))
                for j in range(j0, min(j1, 3 * kts)):
                    kt, term = divmod(j, 3)
                    ins = pe.matmul(bank_[:, :], (wl if term == 2 else wh)[:, s, kt, :],
                                    (rl if term == 1 else rh)(kt),
                                    start=start and j == 0, stop=stop and j == 3 * kts - 1)
                    if j == 3 * kts - 1:
                        ins.then_inc(mm, 1)

            def bank_free(tile_n):
                if not isinstance(tile_n, int) or tile_n >= 2:
                    pe.wait_ge(ev_a, tile_n - 1)
                    pe.wait_ge(ev_d, tile_n - 1)

            def h_h(kt):
                return hh[:, kt, :]

            def h_l(kt):
                return hl[:, kt, :]

            def norm(n, col):
                pe.wait_ge(ssq_s, SSQ_END[n])
                for b in range(QB):
                    ins = pe.matmul(OV[0][:, b:b + 1], ssq[:, b * P:(b + 1) * P], inv_n[:, col:col + 1],
                                    start=True, stop=True)
                ins.then_inc(mean, 1)

            def spread(n):
                pe.wait_ge(diag_s, n + 1)
                pe.matmul(OV[1][:, :], ones[:, :], diag[:, :], start=True, stop=True).then_inc(rb, 1)

            def modulation(k):
                pe.wait_ge(ada_used, AH * (k + 1))
                for t in range(MODT):
                    ins = pe.matmul(OV[1][:, t:t + 1], ada_acc[:, t * P:(t + 1) * P], ones[:, 0:1],
                                    start=True, stop=True)
                ins.then_inc(ada_cols, 1)

            pe.wait_ge(consts, 6)
            pe.wait_ge(vec_in, 16 * 5)
            pe.transpose(TR[0][:, 0:V_ROWS], stage[0:V_ROWS, 0, :], ident[0:V_ROWS, 0:V_ROWS]).then_inc(cols_t, 1)
            for l in range(2):
                pe.wait_ge(conv_in[l], 16 * 4)
                if l == 1:
                    pe.wait_ge(cols_r, 1)
                for j in range(4):
                    ins = pe.transpose(TR[(l + 1) % 2][:, j * 2 * FFT:(j + 1) * 2 * FFT],
                                       stage[0:2 * FFT, 1 + j, :], ident[0:2 * FFT, 0:2 * FFT])
                ins.then_inc(cols_t, 1)
            for t in range(QB):
                pe.wait_ge(x_in[t % 2], 16 * (t // 2 + 1))
                for f in range(2):
                    if t:
                        pe.wait_ge(x_e, 2 * t + f - 1)
                    for q in range(4):
                        kt = 4 * f + q
                        ins = pe.transpose(SC[f][:, q * P:(q + 1) * P], xs[t % 2][:, kt * P:(kt + 1) * P],
                                           ident[:, :])
                    ins.then_inc(x_t, 1)
            modulation(0)
            norm(0, 0)
            spread(0)
            for kt in range(DT):
                pe.wait_ge(h_lo, kt + 1)
                product(C_F, 0, 0, 3 * kt, 3 * kt + 3, h_h, h_l, PJ[T_F % 2])
            for j in range(3):
                bank_free(T_FOX + j)
                product(C_FOX + j, 0, 0, 0, 3 * DT, h_h, h_l, PJ[(T_FOX + j) % 2])
            pe.wait_ge(cum_ok, 2)
            pe.wait_ge(pc, 10)

            def scores(u, unit, rows, par, b, t=None, j=None):
                nc_ = (b + 1) * P
                sc = SC[u % 2][:, 0:nc_]
                q = slice(b * P, (b + 1) * P)
                for term in range(3):
                    pe.matmul(sc, q_tile(gl if term == 2 else gh, par)[rows, q],
                              k_tile(gl if term == 1 else gh, par)[rows, 0:nc_], start=term == 0, stop=False)
                if t is not None:
                    pe.matmul(sc, sel[:, (bass.ds(t * 2 + j, 1) if not isinstance(t, int) else t * 2 + j), :],
                              cum[:, 0:nc_], start=False, stop=False)
                pe.matmul(SC[u % 2][:, b * P:nc_], ident_b[:, :], mask_b[:, :], start=False, stop=True
                          ).then_inc(score, 1)

            def turn(u, unit, b, r, bk, r_of_pair=0):
                pe.wait_ge(pn, unit + 1)
                if r_of_pair:
                    tr_free(r)
                for kb in range(b + 1):
                    ins = pe.transpose(TR[bk][:, kb * P:(kb + 1) * P] if u < QB else
                                       TR[bk][:, (b - kb) * P:(b - kb + 1) * P],
                                       prob[u % 2][:, kb * P:(kb + 1) * P], ident[:, :])
                ins.then_inc(tr_r, 1)

            def tr_free(r):
                pe.wait_ge(tr_lo, r - 1)

            def weighted(h, hd, r_last):
                pe.wait_ge(tr_lo, r_last + 1)
                for kb in range(QB):
                    o = pt_off(h, kb, kb)
                    n = S - kb * P
                    for term in range(3):
                        ins = pe.matmul(OV[h][:, kb * P:S], v_all(gl if term == 2 else gh)[:, kb * P:(kb + 1) * P],
                                        (gl if term == 1 else gh)[:, o:o + n],
                                        start=kb == 0 and term == 0, stop=kb == QB - 1 and term == 2)
                ins.then_inc(pv, 1)

            def fox_pair(i, j, proj, nxt):
                par = j
                U = i * (4 * QB) + (U_FOX + 2 * QB * j)
                R = i * (2 * FOX_TR) + (R_FOX + FOX_TR * j)
                H = i * 4 + (H_FOX + 2 * j)
                n0 = C_FOX + 3 * (j + 1)
                t0 = i * 6 + (T_FOX + 3 * (j + 1))

                def project(a, b):
                    if not proj:
                        return
                    for w in range(3):
                        lo, hi = max(a, 24 * w), min(b, 24 * (w + 1))
                        if lo >= hi:
                            continue
                        if lo == 24 * w:
                            bank_free(t0 + w)
                        product(n0 + w, i, 6, lo - 24 * w, hi - 24 * w, h_h, h_l, PJ[pbank(w, 1 - par)])

                pe.wait_ge(ev_d, i * 6 + (T_FOX + 3 * j + 3))
                for u in range(2 * QB):
                    project(7 * u, 7 * u + 7)
                    rows = slice(u // QB * HD, u // QB * HD + HD)
                    scores(u, U + u, rows, par, u % QB, i * 2 + j, u // QB)
                    if u >= 1:
                        turn(u - 1, U + (u - 1), (u - 1) % QB, R + tr_at(u - 1),
                             (FOX_TR * j + tr_at(u - 1)) % 2, u - 1)
                    if u == 1:
                        for q in range(QB):
                            ins = pe.transpose(TR[(FOX_TR * j + 1) % 2][:, q * P:(q + 1) * P],
                                               vT[:, q * P:(q + 1) * P], ident[:, :])
                        ins.then_inc(tr_r, 1)
                    if u == 5:
                        weighted(0, H, R + tr_at(3))
                project(56, 64)
                turn(7, U + 7, QB - 1, R + tr_at(7), (FOX_TR * j + tr_at(7)) % 2, 7)
                project(64, 72)
                weighted(1, H + 1, R + tr_at(7))

            with pe.Fori(0, PAIRS // 2 - 1) as i:
                for j in range(2):
                    fox_pair(i, j, True, None)
            last = PAIRS // 2 - 1
            fox_pair(last, 0, True, None)
            fox_pair(last, 1, False, None)

            def dense(C, T, heads_done):
                def step(i, j):
                    bank_free(i * 2 + (T + j))
                    product(C + j, i, 2, 0, 3 * DT, lambda kt: tile(gh, kt), lambda kt: tile(gl, kt),
                            PJ[(T + j) % 2])
                pe.wait_ge(o_lo, heads_done)
                with pe.Fori(0, DT // 2) as i:
                    for j in range(2):
                        step(i, j)

            def mlp(l):
                pe.wait_ge(h_lo, DT * (2 * l + 2))
                with pe.Fori(0, FFT // 2) as i:
                    for j in range(4):
                        bank_free(i * 4 + (T_UP[l] + j))
                        product(C_UP[l] + j, i, 4, 0, 3 * DT, h_h, h_l, PJ[(T_UP[l] + j) % 2])
                with pe.Fori(0, DT // 2) as i:
                    for j in range(6):
                        k0 = sum(DOWN_K[:j % 3])
                        if j % 3 == 0:
                            bank_free(i * 2 + (T_DOWN[l] + j // 3))
                        pe.wait_ge(g_lo, FFT * l + k0 + DOWN_K[j % 3])
                        product(C_DOWN[l] + j, i, 6, 0, 3 * DOWN_K[j % 3], lambda kt: tile(gh, k0 + kt),
                                lambda kt: tile(gl, k0 + kt), PJ[(T_DOWN[l] + j // 3) % 2],
                                start=j % 3 == 0, stop=j % 3 == 2)

            dense(C_FOXO, T_FOXO, HEADS)
            modulation(1)
            norm(1, 0)
            spread(1)
            mlp(0)
            modulation(2)
            norm(2, 0)
            spread(2)
            for j in range(QRT + KVRT + 1):
                bank_free(T_MA + j)
                if j == 0:
                    for kt in range(DT):
                        pe.wait_ge(h_lo, DT * 2 + kt + 1)
                        product(C_MA, 0, 0, 3 * kt, 3 * kt + 3, h_h, h_l, PJ[T_MA % 2])
                else:
                    product(C_MA + j, 0, 0, 0, 3 * DT, h_h, h_l, PJ[(T_MA + j) % 2])
                if j == QRT:
                    norm(N_CQ, 1)
            spread(N_CQ)
            pe.wait_ge(dev, N_CQ + 1)
            norm(N_CKV, 2)
            spread(N_CKV)

            def uq_h(kt):
                return hh[:, kt, :]

            def uq_l(kt):
                return hl[:, kt, :]

            def ukv_h(kt):
                return hh[:, QRT + kt, :]

            def ukv_l(kt):
                return hl[:, QRT + kt, :]

            pe.wait_ge(cn_lo, QRT + KVRT)
            bank_free(T_MLA)
            product(C_MLA, 0, 0, 0, 3 * QRT, uq_h, uq_l, PJ[T_MLA % 2])
            bank_free(T_MLA + 1)
            product(C_MLA + 1, 0, 0, 0, 3 * KVRT, ukv_h, ukv_l, PJ[(T_MLA + 1) % 2])

            def mla_head(t, j, proj):
                U = t * (2 * QB) + (U_MLA + QB * j)
                R = t * (2 * MLA_TR) + (R_MLA + MLA_TR * j)
                R0 = R_MLA + MLA_TR * j
                n0 = C_MLA + 2 * (j + 1)
                t0 = t * 4 + (T_MLA + 2 * (j + 1))

                def project(a, b):
                    if not proj:
                        return
                    for w, (s, e, rh, rl) in enumerate(((0, 9, uq_h, uq_l), (9, 15, ukv_h, ukv_l))):
                        lo, hi = max(a, s), min(b, e)
                        if lo >= hi:
                            continue
                        if lo == s:
                            bank_free(t0 + w)
                        product(n0 + w, t, 4, lo - s, hi - s, rh, rl, PJ[(T_MLA + w) % 2])

                pe.wait_ge(ev_d, t * 4 + (T_MLA + 2 * j + 2))
                for b in range(QB):
                    project(3 * b, 3 * b + 3)
                    u = QB * j + b
                    scores(u, U + b, slice(0, MQ), j, b)
                    if b >= 1:
                        turn(u - 1, U + (b - 1), b - 1, R + tr_at(b - 1), (R0 + tr_at(b - 1)) % 2, b - 1)
                    if b == 1:
                        for q in range(QB):
                            ins = pe.transpose(TR[(R0 + 1) % 2][:, q * HD:(q + 1) * HD],
                                               vT[0:HD, q * P:(q + 1) * P], ident[0:HD, 0:HD])
                        ins.then_inc(tr_r, 1)
                project(12, 15)
                turn(QB * j + 3, U + 3, QB - 1, R + tr_at(QB - 1), (R0 + tr_at(QB - 1)) % 2, QB - 1)
                weighted(j, t * 2 + (H_MLA + j), R + tr_at(QB - 1))

            with pe.Fori(0, HEADS // 2 - 1) as t:
                for j in range(2):
                    mla_head(t, j, True)
            mla_head(HEADS // 2 - 1, 0, True)
            mla_head(HEADS // 2 - 1, 1, False)
            dense(C_MLAO, T_MLAO, 2 * HEADS)
            modulation(3)
            norm(5, 0)
            spread(5)
            mlp(1)
            norm(6, 0)
            spread(6)
            pe.wait_ge(fin, DT)
            for t in range(QB):
                for f in range(2):
                    if t:
                        pe.wait_ge(fin_e, 2 * t + f - 1)
                    for q in range(4):
                        kt = 4 * f + q
                        ins = pe.transpose(SC[f][:, q * P:(q + 1) * P], xT[:, kt, t * P:(t + 1) * P],
                                           ident[:, :])
                    ins.then_inc(fin_t, 1)


_INS = ['x', 'c', 'ada_w', 'ada_b', 'fox_w_in', 'fox_b_f', 'fox_w_o', 'mla_w_a', 'mla_g_q', 'mla_g_kv',
        'mla_w_uq', 'mla_w_ukv', 'mla_w_o', 'ffn_w_in', 'ffn_conv_w', 'ffn_conv_b', 'ffn_w_out', 'final_g']


def rope_table():
    freq = np.float32(10000.0) ** (-np.arange(0, ROPE, 2, dtype=np.float32) / np.float32(ROPE))
    ang = (np.arange(S, dtype=np.float32)[:, None] * freq[None, :].astype(np.float32)).T.astype(np.float64)
    cos, sin = np.cos(ang), np.sin(ang)
    return np.concatenate([cos, cos, -sin, sin]).astype(np.float32)


def kernel(**inputs):
    import concourse.bacc as _bacc
    from concourse.bass_utils import run_bass_kernel_spmd as _run

    nc = _bacc.Bacc("TRN2", target_bir_lowering=False, num_devices=1)
    arrays, args = {}, []
    for name in _INS + ['rope']:
        a = rope_table() if name == 'rope' else np.ascontiguousarray(inputs[name])
        arrays[f"in_{name}_dram"] = a
        args.append(nc.dram_tensor(f"in_{name}_dram", a.shape, mybir.dt.from_np(a.dtype),
                                   kind="ExternalInput").ap())
    args.append(nc.dram_tensor("out_0_dram", (1, S, D), F32, kind="ExternalOutput").ap())
    build(nc, *args)
    r = _run(nc, [arrays], core_ids=[0])
    return r.results[0]["out_0_dram"]
```

```python
from contextlib import ExitStack

import numpy as np

import concourse.bass as bass
from concourse import mybir

F32 = mybir.dt.float32
F32R = mybir.dt.float32r
BF16 = mybir.dt.bfloat16
ALU = mybir.AluOpType
ACT = mybir.ActivationFunctionType
AX = mybir.AxisListType

P = 128
D = 1024
DT = D // P
S = 512
QB = S // P
HEADS = 16
HD = 64
PAIRS = HEADS // 2
ROPE = 32
MQ = HD + ROPE
QR, KVR = 384, 256
QRT, KVRT = QR // P, KVR // P
FF = 2816
FFT = FF // P
DOWN_K = (8, 7, 7)
SUBS = 4
MODT = 3 * DT
EPS = 1e-6
FOX_SCALE = float(HD) ** -0.5
MLA_SCALE = float(MQ) ** -0.5
MASKED = -1.0e30

C_F = 0
C_FOX = 1
C_FOXO = C_FOX + 3 * PAIRS
C_UP0 = C_FOXO + DT
C_DOWN0 = C_UP0 + 2 * FFT
C_MA = C_DOWN0 + 3 * DT
C_MLA = C_MA + QRT + KVRT + 1
C_MLAO = C_MLA + 2 * HEADS
C_UP1 = C_MLAO + DT
C_DOWN1 = C_UP1 + 2 * FFT
C_END = C_DOWN1 + 3 * DT
C_UP, C_DOWN = (C_UP0, C_UP1), (C_DOWN0, C_DOWN1)
T_F = 0
T_FOX = 1
T_FOXO = T_FOX + 3 * PAIRS
T_UP0 = T_FOXO + DT
T_DOWN0 = T_UP0 + 2 * FFT
T_MA = T_DOWN0 + DT
T_MLA = T_MA + QRT + KVRT + 1
T_MLAO = T_MLA + 2 * HEADS
T_UP1 = T_MLAO + DT
T_DOWN1 = T_UP1 + 2 * FFT
T_UP, T_DOWN = (T_UP0, T_UP1), (T_DOWN0, T_DOWN1)
U_FOX, U_MLA = 0, HEADS * QB
H_FOX, H_MLA = 0, HEADS
FOX_TR = 2 * QB + 1
MLA_TR = QB + 1
R_FOX = 0
R_MLA = R_FOX + FOX_TR * PAIRS
N_SUB = (0, 1, 2, 5)
N_CQ, N_CKV, N_FINAL = 3, 4, 6
SSQ_TILES = (DT, DT, DT, QRT, KVRT, DT, DT)
SSQ_END = [sum(t + 1 for t in SSQ_TILES[:n + 1]) for n in range(len(SSQ_TILES))]
SQ_END = [sum(SSQ_TILES[:n + 1]) for n in range(len(SSQ_TILES))]
AG = 192
AGN = 3 * D // AG
AK = DT // 2
AH = 2 * AGN
V_C = 0
V_B = V_C + DT
V_GF = V_B + SUBS * MODT
V_GQ = V_GF + DT
V_GKV = V_GQ + QRT
V_ROWS = V_GKV + KVRT


def chunk_k(n):
    if C_MLA <= n < C_MLAO:
        return QRT if (n - C_MLA) % 2 == 0 else KVRT
    for base in C_DOWN:
        if base <= n < base + 3 * DT:
            return DOWN_K[(n - base) % 3]
    return DT


def slot_loads(n):
    if n == C_F:
        return 2
    if n == C_MLA - 1 or (C_MLA <= n < C_MLAO and (n - C_MLA) % 2 == 0):
        return 3
    return 1


def slot_count(n):
    return 16 * sum(slot_loads(c) for c in range(n % 2, n + 1, 2))


def build(nc, x, c, ada_w, ada_b, fox_w_in, fox_b_f, fox_w_o, mla_w_a, mla_g_q, mla_g_kv,
          mla_w_uq, mla_w_ukv, mla_w_o, ffn_w_in, ffn_conv_w, ffn_conv_b, ffn_w_out, final_g,
          rope, out):
    with ExitStack() as ctx:
        def sb(name, shape, dt):
            return ctx.enter_context(nc.sbuf_tensor(name, shape, dt))

        def sem(name):
            return ctx.enter_context(nc.semaphore(name))

        xT = sb("xT", [P, DT, S], F32)
        with nc.sbuf_tensor("first_ada", [P, 6, DT, S], F32) as room:
            first_ada = room
        hh = sb("hh", [P, DT, S], F32R)
        hl = sb("hl", [P, DT, S], F32R)
        gh = sb("gh", [P, FFT * S], F32R)
        gl = sb("gl", [P, FFT * S], F32R)
        raw = sb("raw", [P, 2, DT, P], F32)
        wh = sb("wh", [P, 2, DT, P], F32R)
        wl = sb("wl", [P, 2, DT, P], F32R)
        tmp = sb("tmp", [P, 6, S], F32)
        ssq = sb("ssq", [P, S], F32)
        ada_buf = sb("ada_buf", [P, 2, AK, AG], F32)
        ada_acc = sb("ada_acc", [P, 3 * D], F32)
        ada_part = sb("ada_part", [P, AG], F32)
        sel = sb("sel", [P, HEADS, P], BF16)
        cum = sb("cum", [P, S], BF16)
        rope_sb = sb("rope_sb", [P, S], F32)
        ident = sb("ident", [P, P], F32)
        ident_b = sb("ident_b", [P, P], BF16)
        mask_b = sb("mask_b", [P, P], BF16)
        ones = sb("ones", [P, P], F32)
        inv_n = sb("inv_n", [P, 3], F32)
        cols = sb("cols", [P, V_ROWS], F32)
        conv = sb("conv", [P, 2, 4, 2 * FFT], F32)
        mod = sb("mod", [P, SUBS, MODT], F32)
        csil = sb("csil", [P, DT], F32)
        eps = sb("eps", [P, 1], F32)
        early = sb("early", [P, 8], F32)
        bf_sb = sb("bf_sb", [HEADS, 1], F32)
        diag = sb("diag", [P, S], F32)
        stat = sb("stat", [P, 2, QB], F32)
        nmax = sb("nmax", [P, 8], F32)
        rsum = sb("rsum", [P, 8], F32)
        rinv = sb("rinv", [P, 8], F32)

        def bank(name):
            return ctx.enter_context(nc.psum_tensor(name, [P, S], F32))

        PJ = [bank(f"pj{i}") for i in range(2)]
        SC = [bank(f"sc{i}") for i in range(2)]
        TR = [bank(f"tr{i}") for i in range(2)]
        OV = [bank(f"ov{i}") for i in range(2)]

        def tile(g, t):
            return g[:, t * S:(t + 1) * S] if isinstance(t, int) else g[:, bass.ds(t * S, S)]

        PT0 = DT * S

        def pt_off(h, kb, b):
            return PT0 + ((kb * S + b * P) if h == 0 else ((QB - kb) * S + (b - kb) * P))

        def q_tile(g, par):
            return g[:, (13 + 2 * par) * S:(14 + 2 * par) * S]

        def k_tile(g, par):
            return g[:, (14 + 2 * par) * S:(15 + 2 * par) * S]

        def v_all(g):
            return g[:, 17 * S:18 * S]

        def v_half(g, j):
            return v_all(g).rearrange("p (k d) -> p k d", d=P)[:, :, j * HD:(j + 1) * HD]

        def tr_half(bk):
            return TR[bk][:, 0:QB * HD].rearrange("p (k d) -> p k d", d=HD)

        def pt_view(g, h, b):
            o, step = (PT0 + b * P, S) if h == 0 else (PT0 + (QB - b) * S, S + P)
            return g[:, o:o + step * (b + 1)].rearrange("p (k s) -> p k s", s=step)[:, :, 0:P]

        def tr_at(u):
            return u if u == 0 else u + 1

        def pbank(w, par):
            return (T_FOX + 3 * par + w) % 2

        def ccol(l, tap, f):
            return conv[:, l, tap, f:f + 1] if isinstance(f, int) else conv[:, l, tap, bass.ds(f, 1)]

        def rotate(dve, bk, a, b, out_rows, c):
            dve.tensor_tensor(a, bk[HD:MQ, :], rope_sb[HD:MQ, :], ALU.mult).then_inc(rot, 1)
            dve.tensor_tensor(b, bk[MQ:P, :], rope_sb[MQ:P, :], ALU.mult).then_inc(rot, 1)
            dve.wait_ge(rot, c * 2 + 2)
            dve.tensor_tensor(out_rows, a, b, ALU.add).then_inc(rot_ok, 1)

        prob = [tmp[:, 0, :], tmp[:, 1, :], tmp[:, 5, :], diag[:, :]]
        vT = tmp[:, 2, :]
        rot1, rot2 = tmp[:, 3, :], tmp[:, 4, :]
        fga = [tmp[0:HEADS, i, :] for i in range(6)]
        fgb = tmp[0:HEADS, 3, :].bitcast(BF16)[:, 0:S]
        hpre = [tmp[:, 2 + i, :] for i in range(2)]
        sqb = [tmp[:, i, :] for i in range(2)]

        def first(i):
            return isinstance(i, int) and i == 0

        def turned_unit(i, s):
            return None if first(i) and s < 2 else s - 2

        def done_head(i, s):
            return None if first(i) and s < QB else s // QB - 1

        raw_in = [sem(f"raw_in{i}") for i in range(2)]
        w_hi = sem("w_hi")
        w_lo = sem("w_lo")
        mm = sem("mm")
        ev_a = sem("ev_a")
        ev_d = sem("ev_d")
        vec_in = sem("vec_in")
        conv_in = [sem(f"conv_in{i}") for i in range(2)]
        rest_in = sem("rest_in")
        consts = sem("consts")
        pc = sem("pc")
        cols_t = sem("cols_t")
        cols_r = sem("cols_r")
        x_in = [sem(f"x_in{i}") for i in range(QB)]
        x_t = sem("x_t")
        x_e = sem("x_e")
        ada_in = [sem(f"ada_in{i}") for i in range(2)]
        ada_used = sem("ada_used")
        ada_step = sem("ada_step")
        ada0_in = [sem(f"ada0_in{i}") for i in range(6)]
        ada0_step = sem("ada0_step")
        ada0_sum = sem("ada0_sum")
        gate_cols = sem("gate_cols")
        gate_ok = sem("gate_ok")
        ada_cols = sem("ada_cols")
        mod_pre = sem("mod_pre")
        mod_ok = sem("mod_ok")
        sil = sem("sil")
        sq = sem("sq")
        ssq_s = sem("ssq_s")
        mean = sem("mean")
        dev = sem("dev")
        rstd = sem("rstd")
        diag_s = sem("diag_s")
        rb = sem("rb")
        pre = sem("pre")
        h_hi = sem("h_hi")
        h_lo = sem("h_lo")
        cn_pre = sem("cn_pre")
        cn_hi = sem("cn_hi")
        cn_lo = sem("cn_lo")
        fg_d = sem("fg_d")
        fg_a = sem("fg_a")
        cum_ok = sem("cum_ok")
        score = sem("score")
        nmax_s = sem("nmax_s")
        expd = sem("expd")
        rinv_s = sem("rinv_s")
        pn = sem("pn")
        tr_r = sem("tr_r")
        tr_hi = sem("tr_hi")
        tr_lo = sem("tr_lo")
        pv = sem("pv")
        o_hi = sem("o_hi")
        o_lo = sem("o_lo")
        nope = sem("nope")
        rot = sem("rot")
        rot_ok = sem("rot_ok")
        k_hi = sem("k_hi")
        kr_hi = sem("kr_hi")
        kr_lo = sem("kr_lo")
        tap = sem("tap")
        silu_s = sem("silu_s")
        gate_s = sem("gate_s")
        g_hi = sem("g_hi")
        g_lo = sem("g_lo")
        fin = sem("fin")
        fin_t = sem("fin_t")
        fin_e = sem("fin_e")
        out_s = sem("out_s")

        xs = [tmp[:, 2 * i:2 * i + 2, :].rearrange("p a s -> p (a s)") for i in range(2)] + \
             [ada_acc[:, i * D:(i + 1) * D] for i in range(2)]
        stage = tmp[:, 4:6, :].rearrange("p a (j q) -> p (a j) q", q=P)

        buf_row = ada_buf.rearrange("p h t n -> p (h t n)")
        first_acc = [buf_row[:, i * S:(i + 1) * S] for i in range(3)] + \
                    [ada_acc[:, i * S:(i + 1) * S] for i in (4, 5, 0)]

        block = ctx.enter_context(nc.Block())

        def landed(n0, i, per):
            return slot_count(n0) if not per else i * (slot_count(n0 + per) - slot_count(n0)) + slot_count(n0)

        @block.sync
        def _(sp):
            vec = stage[:, 0, :]
            for src, r0, n in ((c.rearrange("b (t q) -> (b t) q", q=P), V_C, DT),
                               (ada_b.rearrange("l s (t q) -> (l s t) q", q=P), V_B, SUBS * MODT),
                               (final_g.rearrange("(t q) -> t q", q=P), V_GF, DT),
                               (mla_g_q.rearrange("l (t q) -> (l t) q", q=P), V_GQ, QRT),
                               (mla_g_kv.rearrange("l (t q) -> (l t) q", q=P), V_GKV, KVRT)):
                sp.dma_start(vec[r0:r0 + n, :], src).then_inc(vec_in, 16)
            for t in range(QB):
                sp.dma_start(xs[t], x[0, t * P:(t + 1) * P, :]).then_inc(x_in[t], 16)

            def slot_free(n):
                if not isinstance(n, int) or n >= 2:
                    sp.wait_ge(w_hi, n - 1)
                    sp.wait_ge(w_lo, n - 1)

            def load(n0, kt, src, c0=0, c1=P):
                sp.dma_start(raw[:, n0 % 2, 0:kt, c0:c1], src.rearrange("(t p) n -> p t n", p=P)
                             ).then_inc(raw_in[n0 % 2], 16)

            fox = fox_w_in[0]
            load(C_F, DT, fox[:, 3 * D:3 * D + HEADS], 0, HEADS)
            load(C_F, DT, fox[:, 0:P - HEADS], HEADS, P)
            load(C_FOX, DT, fox[:, 0:P])
            sp.dma_start(bf_sb[:, :], fox_b_f.rearrange("l h -> h l")).then_inc(rest_in, 16)
            sp.dma_start(rope_sb[HD:P, :], rope).then_inc(rest_in, 16)
            for l in range(2):
                if l == 1:
                    sp.wait_ge(cols_r, 2)
                for j in range(3):
                    sp.dma_start(stage[0:2 * FFT, 1 + j, :],
                                 ffn_conv_w[l, j].rearrange("(t q) -> t q", q=P)).then_inc(conv_in[l], 16)
                sp.dma_start(stage[0:2 * FFT, 4, :],
                             ffn_conv_b[l].rearrange("(t q) -> t q", q=P)).then_inc(conv_in[l], 16)
            for j in range(1, 6):
                slot_free(C_FOX + j)
                load(C_FOX + j, DT, fox[:, (j % 3) * D + (j // 3) * P:(j % 3) * D + (j // 3 + 1) * P])
            with sp.Fori(0, (PAIRS - 2) // 2) as i:
                for j in range(6):
                    slot_free(i * 6 + (C_FOX + 6 + j))
                    load(C_FOX + j, DT, fox[:, bass.ds(i * (2 * P) + ((2 + j // 3) * P + (j % 3) * D), P)])

            def dense(base, src):
                with sp.Fori(0, DT // 2) as i:
                    for j in range(2):
                        slot_free(i * 2 + (base + j))
                        load(base + j, DT, src[:, bass.ds(i * (2 * P) + j * P, P)])

            def mlp(l):
                with sp.Fori(0, FFT) as i:
                    for j in range(2):
                        slot_free(i * 2 + (C_UP[l] + j))
                        load(C_UP[l] + j, DT, ffn_w_in[l][:, bass.ds(i * P + j * FF, P)])
                with sp.Fori(0, DT // 2) as i:
                    for j in range(6):
                        k0 = sum(DOWN_K[:j % 3]) * P
                        kt = DOWN_K[j % 3]
                        slot_free(i * 6 + (C_DOWN[l] + j))
                        load(C_DOWN[l] + j, kt,
                             ffn_w_out[l][k0:k0 + kt * P, bass.ds(i * (2 * P) + (j // 3) * P, P)])

            dense(C_FOXO, fox_w_o[0])
            mlp(0)
            for j in range(QRT + KVRT):
                slot_free(C_MA + j)
                load(C_MA + j, DT, mla_w_a[0][:, j * P:(j + 1) * P])
            r0 = QR + KVR
            slot_free(C_MLA - 1)
            load(C_MLA - 1, DT, mla_w_a[0][:, r0 - HD:r0 + ROPE], 0, MQ)
            load(C_MLA - 1, DT, mla_w_a[0][:, r0 + ROPE // 2:r0 + ROPE], MQ, MQ + ROPE // 2)
            load(C_MLA - 1, DT, mla_w_a[0][:, r0:r0 + ROPE // 2], MQ + ROPE // 2, P)
            with sp.Fori(0, HEADS) as i:
                slot_free(i * 2 + C_MLA)
                uq = mla_w_uq[0]
                load(C_MLA, QRT, uq[:, bass.ds(i * MQ, MQ)], 0, MQ)
                load(C_MLA, QRT, uq[:, bass.ds(i * MQ + (HD + ROPE // 2), ROPE // 2)], MQ, MQ + ROPE // 2)
                load(C_MLA, QRT, uq[:, bass.ds(i * MQ + HD, ROPE // 2)], MQ + ROPE // 2, P)
                slot_free(i * 2 + (C_MLA + 1))
                load(C_MLA + 1, KVRT, mla_w_ukv[0][:, bass.ds(i * P, P)])
            dense(C_MLAO, mla_w_o[0])
            mlp(1)
            for f in range(2):
                for t in range(QB):
                    sp.wait_ge(fin_e, QB * f + t + 1)
                    sp.dma_start(out[0, t * P:(t + 1) * P, f * S:(f + 1) * S], xs[t][:, f * S:(f + 1) * S]
                                 ).then_inc(out_s, 16)
            sp.wait_ge(out_s, 16 * 2 * QB)

        @block.gpsimd
        def _(pool):
            pool.memset(ident[:, :], 0.0).then_inc(pc, 1)
            pool.memset(ones[:, :], 1.0).then_inc(consts, 1)
            for j, n in enumerate((D, QR, KVR)):
                pool.memset(inv_n[:, j:j + 1], 1.0 / n).then_inc(consts, 1)
            pool.memset(eps[:, :], EPS).then_inc(consts, 1)
            pool.wait_ge(pc, 1)
            pool.affine_select(out=ident[:, :], in_=ident[:, :], compare_op=ALU.not_equal, fill=1.0,
                               base=0, pattern=[[-1, P]], channel_multiplier=1).then_inc(consts, 1)

            def fetch(k, g, half):
                w = ada_w[k // 2, k % 2][half * AK * P:(half + 1) * AK * P, :]
                src = w[:, bass.ds(g * AG, AG)].rearrange("(t p) n -> p t n", p=P)
                pool.dma_start(ada_buf[:, half, :, :], src).then_inc(ada_in[half], 16)

            pool.wait_ge(x_in[1], 16)
            for i in range(6):
                pool.dma_start(first_ada[:, i, :, :], ada_w[0, 0][:, i * S:(i + 1) * S]
                               .rearrange("(t p) n -> p t n", p=P)).then_inc(ada0_in[i], 16)

            for t in (ident_b[:, :], mask_b[:, :], sel[:, :, :], cum[:, :]):
                pool.memset(t, 0.0).then_inc(pc, 1)
            pool.wait_ge(pc, 5)
            pool.affine_select(out=ident_b[:, :], in_=ident_b[:, :], compare_op=ALU.not_equal, fill=1.0,
                               base=0, pattern=[[-1, P]], channel_multiplier=1).then_inc(pc, 1)
            pool.affine_select(out=mask_b[:, :], in_=mask_b[:, :], compare_op=ALU.is_ge, fill=MASKED,
                               base=0, pattern=[[-1, P]], channel_multiplier=1).then_inc(pc, 1)
            for part in range(3):
                pool.wait_ge(pc, 7 + part)
                pool.affine_select(out=sel[:, :, :], in_=sel[:, :, :], compare_op=ALU.not_equal, fill=1.0,
                                   base=-32 * part, pattern=[[-1, HEADS], [0, P]], channel_multiplier=1
                                   ).then_inc(pc, 1)

            def group(k, g, last):
                for half in range(2):
                    buf = ada_buf[:, half, :, :]
                    used = g * 2 + (AH * (k - 1) + half)
                    s0 = g * 5 + (5 * AGN * (k - 1) + 2 * half)
                    pool.wait_ge(ada_in[half], g * 16 + 16 * (AGN * (k - 1) + 1))
                    coef = csil[:, half * AK:(half + 1) * AK].rearrange("p (t o) -> p t o", o=1)
                    pool.tensor_tensor(buf, buf, coef.to_broadcast([P, AK, AG]), ALU.mult).then_inc(ada_step, 1)
                    pool.wait_ge(ada_step, s0 + 1)
                    pool.tensor_tensor(buf[:, 0:2, :], buf[:, 0:2, :], buf[:, 2:4, :], ALU.add
                                       ).then_inc(ada_step, 1)
                    pool.wait_ge(ada_step, s0 + 2)
                    if half == 0:
                        pool.tensor_tensor(ada_part[:, :], buf[:, 0, :], buf[:, 1, :], ALU.add).then_inc(ada_used, 1)
                    else:
                        pool.tensor_tensor(buf[:, 0, :], buf[:, 0, :], buf[:, 1, :], ALU.add
                                           ).then_inc(ada_step, 1)
                        pool.wait_ge(ada_step, s0 + 3)
                        pool.wait_ge(ada_used, used)
                        pool.tensor_tensor(ada_acc[:, bass.ds(g * AG, AG)], ada_part[:, :], buf[:, 0, :],
                                           ALU.add).then_inc(ada_used, 1)
                    if not last:
                        pool.wait_ge(ada_used, used + 1)
                        fetch(k, g + 1, half)

            pool.wait_ge(sil, 1)
            pool.wait_ge(gate_cols, 1)
            for k in range(1, SUBS):
                pool.wait_ge(ada_cols, k)
                for half in range(2):
                    fetch(k, 0, half)
                with pool.Fori(0, AGN - 1) as g:
                    group(k, g, False)
                group(k, AGN - 1, True)

        @block.scalar
        def _(act):
            def split(n0, i=0, per=0):
                kt = chunk_k(n0)
                n = i * per + n0
                act.wait_ge(raw_in[n0 % 2], landed(n0, i, per))
                if per or n0 >= 2:
                    act.wait_ge(mm, n - 1)
                act.activation(wh[:, n0 % 2, 0:kt, :], raw[:, n0 % 2, 0:kt, :], ACT.Copy).then_inc(w_hi, 1)

            def norm(n):
                act.activation(early[:, n:n + 1], eps[:, 0:1], ACT.Sqrt)
                act.wait_ge(mean, n + 1)
                act.activation(stat[:, 0, :], OV[0][:, 0:QB], ACT.Sqrt, bias=eps[:, 0:1]).then_inc(dev, 1)

            def modulated(k):
                act.wait_ge(mod_ok, k + 1)
                for kt in range(DT):
                    act.wait_ge(pre, DT * k + kt + 1)
                    act.activation(hh[:, kt, :], hpre[kt % 2], ACT.Identity,
                                   bias=mod[:, k, kt:kt + 1]).then_inc(h_hi, 1)

            act.wait_ge(cols_t, 1)
            act.activation(cols[:, :], TR[0][:, 0:V_ROWS], ACT.Copy).then_inc(cols_r, 1)
            act.wait_ge(cols_r, 1)
            act.activation(csil[:, :], cols[:, V_C:V_C + DT], ACT.Silu).then_inc(sil, 1)
            for t in range(QB):
                for f in range(2):
                    act.wait_ge(x_t, 2 * t + f + 1)
                    act.activation(xT[:, 4 * f:4 * f + 4, t * P:(t + 1) * P], SC[f][:, :], ACT.Copy
                                   ).then_inc(x_e, 1)
            act.wait_ge(x_e, 2 * QB)
            for kt in range(DT):
                if kt >= 2:
                    act.wait_ge(ssq_s, kt)
                act.activation(sqb[kt % 2], xT[:, kt, :], ACT.Square).then_inc(sq, 1)
            def taps(l):
                act.wait_ge(cols_t, l + 2)
                act.activation(conv[:, l, :, :], TR[1][:, 0:8 * FFT], ACT.Copy).then_inc(cols_r, 1)

            taps(0)
            split(0)
            norm(0)
            split(1)
            taps(1)
            modulated(0)
            split(2)
            act.wait_ge(ev_d, T_F + 1)
            act.activation(fga[2], fga[0], ACT.Abs).then_inc(ev_a, 1)
            act.wait_ge(ev_a, T_F + 1)
            act.activation(fga[3], fga[2], ACT.Exp, scale=-1.0).then_inc(fg_a, 1)
            act.wait_ge(fg_a, 1)
            act.activation(fga[4], fga[3], ACT.Ln, bias=ones[0:HEADS, 0:1]).then_inc(fg_a, 1)

            def fox_q(n, par):
                act.wait_ge(mm, n + 1)
                act.activation(q_tile(gh, par), PJ[pbank(0, par)][:, :], ACT.Copy, scale=FOX_SCALE
                               ).then_inc(ev_a, 1)

            def fox_k(n, par):
                act.wait_ge(mm, n + 1)
                act.activation(k_tile(gh, par), PJ[pbank(1, par)][:, :], ACT.Copy).then_inc(ev_a, 1)

            def fox_v(n, par):
                act.wait_ge(mm, n + 1)
                act.activation(vT[:, 0:S // 2], PJ[pbank(2, par)][:, 0:S // 2], ACT.Copy).then_inc(ev_a, 1)

            for j, take in enumerate((fox_q, fox_k, fox_v)):
                act.wait_ge(mm, C_FOX + j + 1)
                split(C_FOX + j + 2)
                take(C_FOX + j, 0)

            def exp(u, unit):
                nc_ = (u % QB + 1) * P
                act.wait_ge(nmax_s, unit + 1)
                act.activation(prob[u % 4][:, 0:nc_], SC[u % 2][:, 0:nc_], ACT.Exp,
                               bias=nmax[:, u % 8:u % 8 + 1], accum_out=rsum[:, u % 8:u % 8 + 1]
                               ).then_inc(expd, 1)

            def turned(h, b, r, bk):
                act.wait_ge(tr_r, r + 1)
                act.activation(pt_view(gh, h, b), TR[bk][:, 0:(b + 1) * P].rearrange("p (k q) -> p k q", q=P),
                               ACT.Copy).then_inc(tr_hi, 1)

            def o_take(h, t, hd):
                act.wait_ge(pv, hd + 1)
                rows = slice(h * HD, (h + 1) * HD)
                act.activation(tile(gh, t)[rows, :], OV[h][rows, :], ACT.Copy).then_inc(o_hi, 1)

            def fox_step(i, s, fill, nxt):
                j, u = s // 8, s % 8
                R = i * (2 * FOX_TR) + R_FOX
                n0 = C_FOX + 3 * (j + 1)
                v = turned_unit(i, s)
                if v is not None and v < 16:
                    r = FOX_TR * (v // 8) + tr_at(v % 8)
                    turned(v // QB % 2, v % QB, R + r, r % 2)
                if s < 16:
                    exp(s, i * 16 + (U_FOX + s))
                if s < 16 and u == 2:
                    act.wait_ge(tr_r, R + (FOX_TR * j + 2))
                    act.activation(v_all(gh), TR[(FOX_TR * j + 1) % 2][:, :], ACT.Copy).then_inc(tr_hi, 1)
                h = done_head(i, s)
                if u % QB == 3 and h is not None:
                    o_take(h % 2, i * 2 + h // 2, i * 4 + (H_FOX + h))
                if fill and u == 2:
                    split_after(n0, i, 6, nxt)
                    fox_q(i * 6 + n0, 1 - j)
                if fill and u == 5:
                    split_after(n0 + 1, i, 6, nxt)
                    fox_k(i * 6 + (n0 + 1), 1 - j)
                if fill and u == 7:
                    split_after(n0 + 2, i, 6, nxt)
                    fox_v(i * 6 + (n0 + 2), 1 - j)

            def split_after(n0, i, per, nxt):
                act.wait_ge(mm, i * per + (n0 + 1))
                if nxt is None:
                    split(n0 + 2, i, per)
                else:
                    split(nxt + n0 + 2)

            for s in range(16):
                fox_step(0, s, True, None)
            last = PAIRS // 2 - 1
            with act.Fori(1, last) as i:
                for s in range(16):
                    fox_step(i, s, True, None)
            for s in range(20):
                fox_step(last, s, s < 8, 6 * last)

            def residual(m, tile0, norm_n, j):
                act.wait_ge(ev_d, tile0 + 1)
                act.wait_ge(ssq_s, m + SSQ_END[norm_n - 1])
                src = xT[:, m, :] if isinstance(m, int) else xT[:, bass.ds(m, 1), :]
                act.activation(sqb[j % 2], src, ACT.Square).then_inc(ev_a, 1)

            def dense(C, T, norm_n):
                def step(i, j, nxt):
                    split_after(C + j, i, 2, nxt)
                    residual(i * 2 + j, i * 2 + (T + j), norm_n, j)
                with act.Fori(0, DT // 2 - 1) as i:
                    for j in range(2):
                        step(i, j, None)
                for j in range(2):
                    step(DT // 2 - 1, j, DT - 2)

            def mlp(l, norm_n):
                C, T = C_UP[l], T_UP[l]

                def pair(i, par, nxt):
                    m = i * 2 + par
                    for side, y in ((0, tmp[:, par, :]), (1, tmp[:, 2 + par, :])):
                        j = 2 * par + side
                        split_after(C + j, i, 4, nxt)
                        f = m + side * FFT
                        act.activation(y, PJ[(T + j) % 2][:, :], ACT.Identity, bias=ccol(l, 3, f),
                                       scale=ccol(l, 2, f)).then_inc(ev_a, 1)
                    act.wait_ge(ev_d, i * 4 + (T + 2 * par + 1))
                    act.activation(tmp[:, par, :], tmp[:, par, :], ACT.Silu).then_inc(silu_s, 1)
                    act.wait_ge(gate_s, m + (FFT * l + 1))
                    act.activation(tile(gh, m), tmp[:, 2 + par, :], ACT.Copy).then_inc(g_hi, 1)

                with act.Fori(0, FFT // 2 - 1) as i:
                    act.activation(early[:, 7:8], eps[:, 0:1], ACT.Silu)
                    for par in range(2):
                        pair(i, par, None)
                for par in range(2):
                    pair(FFT // 2 - 1, par, 4 * (FFT // 2 - 1))

                C, T = C_DOWN[l], T_DOWN[l]

                def down(i, nxt):
                    for j in range(6):
                        if nxt is not None and C + nxt + j + 2 >= C_END:
                            act.wait_ge(mm, C + nxt + j + 1)
                        else:
                            split_after(C + j, i, 6, nxt)
                        if j % 3 == 2:
                            residual(i * 2 + j // 3, i * 2 + (T + j // 3), norm_n, j // 3)
                with act.Fori(0, DT // 2 - 1) as i:
                    down(i, None)
                down(DT // 2 - 1, 6 * (DT // 2 - 1))

            dense(C_FOXO, T_FOXO, 1)
            norm(1)
            modulated(1)
            mlp(0, 2)
            norm(2)
            modulated(2)
            for j in range(QRT + KVRT + 1):
                act.wait_ge(mm, C_MA + j + 1)
                split(C_MA + j + 2)
                if j < QRT + KVRT:
                    done = SSQ_END[N_CQ - 1] + 1 + j + (1 if j >= QRT else 0)
                    if j > 0:
                        act.wait_ge(ssq_s, done - (1 if j == QRT else 0))
                    act.activation(tmp[:, 5, :], PJ[(T_MA + j) % 2][:, :], ACT.Square).then_inc(ev_a, 1)
                    if j == QRT:
                        norm(N_CQ)
                else:
                    act.wait_ge(rot_ok, 1)
                    for par in range(2):
                        act.activation(k_tile(gh, par)[HD:MQ, :], tmp[HD:MQ, 5, :], ACT.Copy
                                       ).then_inc(ev_a if par else kr_hi, 1)
            norm(N_CKV)
            for j in range(QRT + KVRT):
                act.wait_ge(cn_pre, j + 1)
                act.activation(hh[:, j, :], tmp[:, j, :], ACT.Copy).then_inc(cn_hi, 1)

            def mla_nope(n_q):
                act.wait_ge(mm, n_q + 1)
                act.activation(rot1[0:HD, :], PJ[T_MLA % 2][0:HD, :], ACT.Copy).then_inc(nope, 1)

            def mla_take(h, par):
                act.wait_ge(nope, h + 1)
                act.wait_ge(rot_ok, h + 2)
                act.activation(q_tile(gh, par)[0:MQ, :], rot1[0:MQ, :], ACT.Copy, scale=MLA_SCALE
                               ).then_inc(ev_a, 1)

            def mla_take_kv(par, n_kv):
                act.wait_ge(mm, n_kv + 1)
                act.activation(k_tile(gh, par)[0:HD, :], PJ[(T_MLA + 1) % 2][0:HD, :], ACT.Copy).then_inc(k_hi, 1)
                act.activation(vT[0:HD, :], PJ[(T_MLA + 1) % 2][HD:P, :], ACT.Copy).then_inc(ev_a, 1)

            split_after(C_MLA, 0, 0, 0)
            mla_nope(C_MLA)
            mla_take(0, 0)
            split_after(C_MLA + 1, 0, 0, 0)
            mla_take_kv(0, C_MLA + 1)

            def mla_step(t, s, fill, nxt):
                j, b = s // QB, s % QB
                R = t * (2 * MLA_TR) + R_MLA
                n0 = C_MLA + 2 * (j + 1)
                v = turned_unit(t, s)
                if v is not None and v < 8:
                    r = MLA_TR * (v // QB) + tr_at(v % QB)
                    turned(v // QB % 2, v % QB, R + r, (R_MLA + r) % 2)
                if s < 8:
                    exp(s, t * 8 + (U_MLA + s))
                if s < 8 and b == 2:
                    act.wait_ge(tr_r, R + (MLA_TR * j + 2))
                    act.activation(v_half(gh, j), tr_half((R_MLA + MLA_TR * j + 1) % 2), ACT.Copy
                                   ).then_inc(tr_hi, 1)
                h = done_head(t, s)
                if b == 3 and h is not None:
                    o_take(h % 2, t + h // 2, t * 2 + (H_MLA + h))
                if fill and b == 1:
                    split_after(n0, t, 4, nxt)
                    mla_nope(t * 4 + n0)
                if fill and b == 2:
                    mla_take(t * 2 + (j + 1), 1 - j)
                    split_after(n0 + 1, t, 4, nxt)
                    mla_take_kv(1 - j, t * 4 + (n0 + 1))

            for s in range(8):
                mla_step(0, s, True, None)
            last = HEADS // 2 - 1
            with act.Fori(1, last) as t:
                for s in range(8):
                    mla_step(t, s, True, None)
            for s in range(12):
                mla_step(last, s, s < QB, 4 * last)
            dense(C_MLAO, T_MLAO, 5)
            norm(5)
            modulated(3)
            mlp(1, 6)
            norm(6)
            for f in range(2):
                for t in range(QB):
                    act.wait_ge(fin_t, QB * f + t + 1)
                    act.activation(xs[t][:, f * S:(f + 1) * S], SC[t % 2][:, :], ACT.Copy).then_inc(fin_e, 1)

        @block.vector
        def _(dve):
            def f32(ap):
                return ap.bitcast(F32)

            def split(n0, i=0, per=0):
                kt = chunk_k(n0)
                dve.wait_ge(w_hi, i * per + (n0 + 1))
                dve.tensor_tensor(wl[:, n0 % 2, 0:kt, :], raw[:, n0 % 2, 0:kt, :],
                                  f32(wh[:, n0 % 2, 0:kt, :]), ALU.subtract).then_inc(w_lo, 1)

            def split_after(n0, i, per, nxt):
                if nxt is None:
                    split(n0 + 2, i, per)
                elif nxt + n0 + 2 < C_END:
                    split(nxt + n0 + 2)

            def modulation(k):
                dve.wait_ge(ada_cols, k + 1)
                dve.tensor_tensor(mod[:, k, :], SC[0][:, 0:MODT],
                                  cols[:, V_B + MODT * k:V_B + MODT * (k + 1)], ALU.add).then_inc(mod_pre, 1)
                dve.wait_ge(mod_pre, k + 1)
                dve.tensor_scalar(mod[:, k, DT:2 * DT], mod[:, k, DT:2 * DT], 1.0, None, ALU.add
                                  ).then_inc(mod_ok, 1)

            def norm(n):
                dve.wait_ge(dev, n + 1)
                if n:
                    dve.wait_ge(diag_s, n)
                dve.reciprocal(stat[:, 1, :], stat[:, 0, :]).then_inc(rstd, 1)
                dve.wait_ge(rstd, n + 1)
                for b in range(QB):
                    ins = dve.tensor_scalar(diag[:, b * P:(b + 1) * P], ident[:, :], stat[:, 1, b:b + 1],
                                            None, ALU.mult)
                ins.then_inc(diag_s, 1)

            def modulated(k, norm_n):
                dve.wait_ge(mod_ok, k + 1)
                dve.wait_ge(rb, norm_n + 1)

                def low(kt):
                    dve.wait_ge(h_hi, DT * k + kt + 1)
                    dve.scalar_tensor_tensor(out=hl[:, kt, :], in0=hpre[kt % 2], scalar=mod[:, k, kt:kt + 1],
                                             in1=f32(hh[:, kt, :]), op0=ALU.add, op1=ALU.subtract
                                             ).then_inc(h_lo, 1)
                for kt in range(DT):
                    if kt >= 2:
                        dve.wait_ge(h_lo, DT * k + kt - 1)
                    dve.scalar_tensor_tensor(out=hpre[kt % 2], in0=xT[:, kt, :],
                                             scalar=mod[:, k, DT + kt:DT + kt + 1], in1=OV[1][:, :],
                                             op0=ALU.mult, op1=ALU.mult).then_inc(pre, 1)
                    if kt:
                        low(kt - 1)
                low(DT - 1)

            def first_modulation(i):
                dve.wait_ge(ada0_in[i], 16)
                acc = first_acc[i]
                for kt in range(DT):
                    w = first_ada[:, i, kt, :]
                    if kt == 0:
                        dve.tensor_scalar(acc, w, csil[:, 0:1], None, ALU.mult).then_inc(ada0_step, 1)
                        continue
                    dve.wait_ge(ada0_step, (DT - 1) * i + kt)
                    dve.scalar_tensor_tensor(out=acc, in0=w, scalar=csil[:, kt:kt + 1], in1=acc,
                                             op0=ALU.mult, op1=ALU.add
                                             ).then_inc(ada0_sum if kt == DT - 1 else ada0_step, 1)

            dve.wait_ge(sil, 1)
            first_modulation(0)
            dve.memset(ssq[:, :], 0.0).then_inc(ssq_s, 1)
            for kt in range(DT):
                dve.wait_ge(sq, kt + 1)
                dve.wait_ge(ssq_s, kt + 1)
                dve.tensor_tensor(ssq[:, :], ssq[:, :], sqb[kt % 2], ALU.add).then_inc(ssq_s, 1)
            first_modulation(1)
            norm(0)
            split(0)
            first_modulation(2)
            split(1)
            first_modulation(3)
            dve.wait_ge(ada_cols, 1)
            dve.tensor_tensor(mod[:, 0, 0:2 * DT], TR[0][:, 0:2 * DT], cols[:, V_B:V_B + 2 * DT], ALU.add
                              ).then_inc(mod_pre, 1)
            dve.wait_ge(mod_pre, 1)
            dve.tensor_scalar(mod[:, 0, DT:2 * DT], mod[:, 0, DT:2 * DT], 1.0, None, ALU.add
                              ).then_inc(mod_ok, 1)
            modulated(0, 0)
            split(2)
            dve.memset(fga[5], 1.0).then_inc(fg_d, 1)
            dve.wait_ge(mm, C_F + 1)
            dve.wait_ge(rest_in, 32)
            dve.tensor_scalar(fga[0], PJ[T_F % 2][0:HEADS, :], bf_sb[:, 0:1], None, ALU.add).then_inc(ev_d, 1)
            dve.wait_ge(ev_d, T_F + 1)
            dve.tensor_scalar(fga[1], fga[0], 0.0, None, ALU.min).then_inc(fg_d, 1)
            dve.wait_ge(fg_d, 2)
            dve.wait_ge(fg_a, 2)
            dve.tensor_tensor(fga[4], fga[4], fga[1], ALU.subtract).then_inc(fg_d, 1)
            dve.wait_ge(fg_d, 3)
            dve.tensor_tensor_scan(fga[0], fga[5], fga[4], 0.0, ALU.mult, ALU.add).then_inc(fg_d, 1)
            dve.wait_ge(fg_d, 4)
            dve.wait_ge(pc, 10)
            dve.tensor_copy(cum[0:HEADS, :], fga[0]).then_inc(fg_d, 1)
            dve.wait_ge(fg_d, 5)
            dve.tensor_tensor(fga[1], fga[0], cum[0:HEADS, :], ALU.subtract).then_inc(fg_d, 1)
            dve.wait_ge(fg_d, 6)
            dve.tensor_copy(fgb, fga[1]).then_inc(fg_d, 1)
            dve.wait_ge(fg_d, 7)
            dve.tensor_copy(cum[32:32 + HEADS, :], fgb).then_inc(cum_ok, 1)
            dve.tensor_tensor(fga[4], fga[1], fgb, ALU.subtract).then_inc(fg_d, 1)
            dve.wait_ge(fg_d, 8)
            dve.tensor_copy(cum[64:64 + HEADS, :], fga[4]).then_inc(cum_ok, 1)

            def fox_q(n_tile, par):
                dve.wait_ge(ev_a, n_tile + 1)
                dve.scalar_tensor_tensor(out=q_tile(gl, par), in0=PJ[pbank(0, par)][:, :], scalar=FOX_SCALE,
                                         in1=f32(q_tile(gh, par)), op0=ALU.mult, op1=ALU.subtract
                                         ).then_inc(ev_d, 1)

            def fox_k(n_tile, par):
                dve.wait_ge(ev_a, n_tile + 1)
                dve.tensor_tensor(k_tile(gl, par), PJ[pbank(1, par)][:, :], f32(k_tile(gh, par)), ALU.subtract
                                  ).then_inc(ev_d, 1)

            def fox_v(n_tile, par):
                dve.wait_ge(ev_a, n_tile + 1)
                dve.tensor_copy(vT[:, S // 2:S], PJ[pbank(2, par)][:, S // 2:S]).then_inc(ev_d, 1)

            for j, take in enumerate((fox_q, fox_k, fox_v)):
                split(C_FOX + j + 2)
                take(T_FOX + j, 0)
                if j < 2:
                    first_modulation(4 + j)
            dve.wait_ge(gate_cols, 1)
            dve.tensor_tensor(mod[:, 0, 2 * DT:MODT], TR[1][:, 0:DT], cols[:, V_B + 2 * DT:V_B + MODT],
                              ALU.add).then_inc(gate_ok, 1)

            def maximum(u, unit):
                nc_ = (u % QB + 1) * P
                dve.wait_ge(score, unit + 1)
                dve.tensor_reduce(nmax[:, u % 8:u % 8 + 1], SC[u % 2][:, 0:nc_], AX.X, ALU.max, negate=True
                                  ).then_inc(nmax_s, 1)

            def normalise(u, unit):
                nc_ = (u % QB + 1) * P
                c = slice(u % 8, u % 8 + 1)
                dve.wait_ge(expd, unit + 1)
                dve.reciprocal(rinv[:, c], rsum[:, c]).then_inc(rinv_s, 1)
                dve.wait_ge(rinv_s, unit + 1)
                dve.tensor_scalar(prob[u % 4][:, 0:nc_], prob[u % 4][:, 0:nc_], rinv[:, c], None,
                                  ALU.mult).then_inc(pn, 1)

            def turned(h, b, r, bk):
                dve.wait_ge(tr_hi, r + 1)
                dve.tensor_tensor(pt_view(gl, h, b), TR[bk][:, 0:(b + 1) * P].rearrange("p (k q) -> p k q", q=P),
                                  f32(pt_view(gh, h, b)), ALU.subtract).then_inc(tr_lo, 1)

            def o_take(h, t, hd):
                dve.wait_ge(o_hi, hd + 1)
                rows = slice(h * HD, (h + 1) * HD)
                dve.tensor_tensor(tile(gl, t)[rows, :], OV[h][rows, :], f32(tile(gh, t)[rows, :]), ALU.subtract
                                  ).then_inc(o_lo, 1)

            def fox_step(i, s, fill, nxt):
                j, u = s // 8, s % 8
                R = i * (2 * FOX_TR) + R_FOX
                n0 = C_FOX + 3 * (j + 1)
                t0 = i * 6 + (T_FOX + 3 * (j + 1))
                if s < 16:
                    maximum(s, i * 16 + (U_FOX + s))
                if s <= 16 and (s or not first(i)):
                    normalise(s - 1, i * 16 + (U_FOX + s - 1))
                if s < 16 and u == 3:
                    dve.wait_ge(tr_hi, R + (FOX_TR * j + 2))
                    dve.tensor_tensor(v_all(gl), TR[(FOX_TR * j + 1) % 2][:, :], f32(v_all(gh)),
                                      ALU.subtract).then_inc(tr_lo, 1)
                v = turned_unit(i, s)
                if v is not None and v < 16:
                    r = FOX_TR * (v // 8) + tr_at(v % 8)
                    turned(v // QB % 2, v % QB, R + r, r % 2)
                h = done_head(i, s)
                if u % QB == 3 and h is not None:
                    o_take(h % 2, i * 2 + h // 2, i * 4 + (H_FOX + h))
                if fill and u == 2:
                    split_after(n0, i, 6, nxt)
                    fox_q(t0, 1 - j)
                if fill and u == 5:
                    split_after(n0 + 1, i, 6, nxt)
                    fox_k(t0 + 1, 1 - j)
                if fill and u == 7:
                    split_after(n0 + 2, i, 6, nxt)
                    fox_v(t0 + 2, 1 - j)

            for s in range(16):
                fox_step(0, s, True, None)
            last = PAIRS // 2 - 1
            with dve.Fori(1, last) as i:
                for s in range(16):
                    fox_step(i, s, True, None)
            for s in range(20):
                fox_step(last, s, s < 8, 6 * last)

            def xtile(m):
                return xT[:, m, :] if isinstance(m, int) else xT[:, bass.ds(m, 1), :]

            def residual(m, j, tile_n, bk, k, norm_n):
                g = mod[:, k, 2 * DT + m:2 * DT + m + 1] if isinstance(m, int) else \
                    mod[:, k, bass.ds(m + 2 * DT, 1)]
                dve.scalar_tensor_tensor(out=xtile(m), in0=PJ[bk][:, :], scalar=g, in1=xtile(m),
                                         op0=ALU.mult, op1=ALU.add).then_inc(ev_d, 1)
                dve.wait_ge(ev_a, tile_n + 1)
                dve.wait_ge(ssq_s, m + (SSQ_END[norm_n - 1] + 1))
                dve.tensor_tensor(ssq[:, :], ssq[:, :], sqb[j % 2], ALU.add).then_inc(ssq_s, 1)

            def dense(C, T, k, norm_n):
                def step(i, j, nxt):
                    split_after(C + j, i, 2, nxt)
                    dve.wait_ge(mm, i * 2 + (C + j + 1))
                    residual(i * 2 + j, j, i * 2 + (T + j), (T + j) % 2, k, norm_n)
                dve.memset(ssq[:, :], 0.0).then_inc(ssq_s, 1)
                with dve.Fori(0, DT // 2 - 1) as i:
                    for j in range(2):
                        step(i, j, None)
                for j in range(2):
                    step(DT // 2 - 1, j, DT - 2)

            def mlp(l, k, norm_n):
                C, T = C_UP[l], T_UP[l]

                def pair(i, par, nxt):
                    m = i * 2 + par
                    yg, yv = tmp[:, par, :], tmp[:, 2 + par, :]
                    for side, y in ((0, yg), (1, yv)):
                        j = 2 * par + side
                        bk = PJ[(T + j) % 2]
                        f = m + side * FFT
                        split_after(C + j, i, 4, nxt)
                        dve.wait_ge(ev_a, i * 4 + (T + j + 1))
                        dve.scalar_tensor_tensor(out=y[:, 1:S], in0=bk[:, 0:S - 1], scalar=ccol(l, 1, f),
                                                 in1=y[:, 1:S], op0=ALU.mult, op1=ALU.add).then_inc(tap, 1)
                        dve.wait_ge(tap, i * 4 + (2 * FFT * l + j + 1))
                        dve.scalar_tensor_tensor(out=y[:, 2:S], in0=bk[:, 0:S - 2], scalar=ccol(l, 0, f),
                                                 in1=y[:, 2:S], op0=ALU.mult, op1=ALU.add).then_inc(ev_d, 1)
                    dve.wait_ge(silu_s, m + (FFT * l + 1))
                    dve.wait_ge(ev_d, i * 4 + (T + 2 * par + 2))
                    dve.tensor_tensor(yv, yg, yv, ALU.mult).then_inc(gate_s, 1)
                    dve.wait_ge(g_hi, m + (FFT * l + 1))
                    dve.tensor_tensor(tile(gl, m), yv, f32(tile(gh, m)), ALU.subtract).then_inc(g_lo, 1)

                with dve.Fori(0, FFT // 2 - 1) as i:
                    for par in range(2):
                        pair(i, par, None)
                for par in range(2):
                    pair(FFT // 2 - 1, par, 4 * (FFT // 2 - 1))

                C, T = C_DOWN[l], T_DOWN[l]

                def down(i, nxt):
                    for j in range(6):
                        split_after(C + j, i, 6, nxt)
                        if j % 3 == 2:
                            dve.wait_ge(mm, i * 6 + (C + j + 1))
                            residual(i * 2 + j // 3, j // 3, i * 2 + (T + j // 3), (T + j // 3) % 2, k, norm_n)
                dve.memset(ssq[:, :], 0.0).then_inc(ssq_s, 1)
                with dve.Fori(0, DT // 2 - 1) as i:
                    down(i, None)
                down(DT // 2 - 1, 6 * (DT // 2 - 1))

            modulation(1)
            dve.wait_ge(gate_ok, 1)
            dense(C_FOXO, T_FOXO, 0, 1)
            norm(1)
            modulated(1, 1)
            mlp(0, 1, 2)
            norm(2)
            modulation(2)
            modulated(2, 2)
            s0 = SSQ_END[N_CQ - 1]
            dve.memset(ssq[:, :], 0.0).then_inc(ssq_s, 1)
            for j in range(QRT + KVRT + 1):
                bk = PJ[(T_MA + j) % 2]
                split(C_MA + j + 2)
                dve.wait_ge(ev_a, T_MA + j + 1) if j < QRT + KVRT else dve.wait_ge(mm, C_MA + j + 1)
                if j < QRT + KVRT:
                    dve.tensor_copy(tmp[:, j, :], bk[:, :]).then_inc(ev_d, 1)
                    extra = 1
                    if j == QRT:
                        dve.wait_ge(mean, N_CQ + 1)
                        dve.memset(ssq[:, :], 0.0).then_inc(ssq_s, 1)
                    if j >= QRT:
                        extra = 2
                    dve.wait_ge(ssq_s, s0 + j + extra)
                    dve.tensor_tensor(ssq[:, :], ssq[:, :], tmp[:, 5, :], ALU.add).then_inc(ssq_s, 1)
                    if j == QRT:
                        norm(N_CQ)
                else:
                    dve.wait_ge(ssq_s, SSQ_END[N_CKV])
                    rotate(dve, bk, tmp[0:ROPE, 5, :], rope_sb[0:ROPE, :], tmp[HD:MQ, 5, :], 0)
                    dve.wait_ge(kr_hi, 1)
                    dve.tensor_tensor(k_tile(gl, 0)[HD:MQ, :], tmp[HD:MQ, 5, :],
                                      f32(k_tile(gh, 0)[HD:MQ, :]), ALU.subtract).then_inc(kr_lo, 1)
                    dve.wait_ge(ev_a, T_MA + j + 1)
                    dve.tensor_tensor(k_tile(gl, 1)[HD:MQ, :], tmp[HD:MQ, 5, :],
                                      f32(k_tile(gh, 1)[HD:MQ, :]), ALU.subtract).then_inc(ev_d, 1)

            def latent(j, n, gcol):
                dve.wait_ge(rb, n + 1)
                dve.scalar_tensor_tensor(out=tmp[:, j, :], in0=tmp[:, j, :], scalar=cols[:, gcol:gcol + 1],
                                         in1=OV[1][:, :], op0=ALU.mult, op1=ALU.mult).then_inc(cn_pre, 1)

            dve.wait_ge(ev_d, T_MA + QRT + KVRT)
            for j in range(QRT):
                latent(j, N_CQ, V_GQ + j)
            norm(N_CKV)
            for j in range(KVRT):
                latent(QRT + j, N_CKV, V_GKV + j)
            for j in range(QRT + KVRT):
                dve.wait_ge(cn_hi, j + 1)
                dve.tensor_tensor(hl[:, j, :], tmp[:, j, :], f32(hh[:, j, :]), ALU.subtract).then_inc(cn_lo, 1)

            def mla_rotate(h, n_q):
                dve.wait_ge(mm, n_q + 1)
                rotate(dve, PJ[T_MLA % 2], rot1[HD:MQ, :], rot2[HD:MQ, :], rot1[HD:MQ, :], h + 1)

            def mla_take(par, tile_q):
                dve.wait_ge(ev_a, tile_q + 1)
                dve.scalar_tensor_tensor(out=q_tile(gl, par)[0:MQ, :], in0=rot1[0:MQ, :], scalar=MLA_SCALE,
                                         in1=f32(q_tile(gh, par)[0:MQ, :]), op0=ALU.mult, op1=ALU.subtract
                                         ).then_inc(ev_d, 1)

            def mla_take_kv(h, par, tile_kv):
                dve.wait_ge(ev_a, tile_kv + 1)
                dve.wait_ge(k_hi, h + 1)
                dve.tensor_tensor(k_tile(gl, par)[0:HD, :], PJ[(T_MLA + 1) % 2][0:HD, :],
                                  f32(k_tile(gh, par)[0:HD, :]), ALU.subtract).then_inc(ev_d, 1)

            split_after(C_MLA, 0, 0, 0)
            mla_rotate(0, C_MLA)
            mla_take(0, T_MLA)
            split_after(C_MLA + 1, 0, 0, 0)
            mla_take_kv(0, 0, T_MLA + 1)

            def mla_step(t, s, fill, nxt):
                j, b = s // QB, s % QB
                R = t * (2 * MLA_TR) + R_MLA
                n0 = C_MLA + 2 * (j + 1)
                t0 = t * 4 + (T_MLA + 2 * (j + 1))
                if s < 8:
                    maximum(s, t * 8 + (U_MLA + s))
                if s <= 8 and (s or not first(t)):
                    normalise(s - 1, t * 8 + (U_MLA + s - 1))
                if s < 8 and b == 3:
                    dve.wait_ge(tr_hi, R + (MLA_TR * j + 2))
                    dve.tensor_tensor(v_half(gl, j), tr_half((R_MLA + MLA_TR * j + 1) % 2),
                                      f32(v_half(gh, j)), ALU.subtract).then_inc(tr_lo, 1)
                v = turned_unit(t, s)
                if v is not None and v < 8:
                    r = MLA_TR * (v // QB) + tr_at(v % QB)
                    turned(v // QB % 2, v % QB, R + r, (R_MLA + r) % 2)
                h = done_head(t, s)
                if b == 3 and h is not None:
                    o_take(h % 2, t + h // 2, t * 2 + (H_MLA + h))
                if fill and b == 1:
                    split_after(n0, t, 4, nxt)
                    mla_rotate(t * 2 + (j + 1), t * 4 + n0)
                if fill and b == 2:
                    mla_take(1 - j, t0)
                    split_after(n0 + 1, t, 4, nxt)
                    mla_take_kv(t * 2 + (j + 1), 1 - j, t0 + 1)

            for s in range(8):
                mla_step(0, s, True, None)
            last = HEADS // 2 - 1
            with dve.Fori(1, last) as t:
                for s in range(8):
                    mla_step(t, s, True, None)
            for s in range(12):
                mla_step(last, s, s < QB, 4 * last)
            modulation(3)
            dense(C_MLAO, T_MLAO, 2, 5)
            norm(5)
            modulated(3, 5)
            mlp(1, 3, 6)
            norm(6)
            dve.wait_ge(rb, N_FINAL + 1)
            for kt in range(DT):
                dve.scalar_tensor_tensor(out=xT[:, kt, :], in0=xT[:, kt, :],
                                         scalar=cols[:, V_GF + kt:V_GF + kt + 1], in1=OV[1][:, :],
                                         op0=ALU.mult, op1=ALU.mult).then_inc(fin, 1)

        @block.tensor
        def _(pe):
            def product(n0, i, per, j0, j1, rh, rl, bank_, start=True, stop=True):
                s = n0 % 2
                kts = chunk_k(n0)
                if j0 == 0:
                    pe.wait_ge(w_hi, i * per + (n0 + 1))
                    pe.wait_ge(w_lo, i * per + (n0 + 1))
                for j in range(j0, min(j1, 3 * kts)):
                    kt, term = divmod(j, 3)
                    ins = pe.matmul(bank_[:, :], (wl if term == 2 else wh)[:, s, kt, :],
                                    (rl if term == 1 else rh)(kt),
                                    start=start and j == 0, stop=stop and j == 3 * kts - 1)
                    if j == 3 * kts - 1:
                        ins.then_inc(mm, 1)

            def bank_free(tile_n):
                if not isinstance(tile_n, int) or tile_n >= 2:
                    pe.wait_ge(ev_a, tile_n - 1)
                    pe.wait_ge(ev_d, tile_n - 1)

            def h_h(kt):
                return hh[:, kt, :]

            def h_l(kt):
                return hl[:, kt, :]

            def two_tiles(C, T, h0):
                for kt in range(DT):
                    pe.wait_ge(h_lo, h0 + kt + 1)
                    for j in range(2):
                        if kt == 0:
                            bank_free(T + j)
                        product(C + j, 0, 0, 3 * kt, 3 * kt + 3, h_h, h_l, PJ[(T + j) % 2])

            def norm(n, col):
                pe.wait_ge(ssq_s, SSQ_END[n])
                for b in range(QB):
                    ins = pe.matmul(OV[0][:, b:b + 1], ssq[:, b * P:(b + 1) * P], inv_n[:, col:col + 1],
                                    start=True, stop=True)
                ins.then_inc(mean, 1)

            def spread(n):
                pe.wait_ge(diag_s, n + 1)
                pe.matmul(OV[1][:, :], ones[:, :], diag[:, :], start=True, stop=True).then_inc(rb, 1)

            def modulation(k):
                pe.wait_ge(ada_used, AH * k)
                for t in range(MODT):
                    ins = pe.matmul(SC[0][:, t:t + 1], ada_acc[:, t * P:(t + 1) * P], ones[:, 0:1],
                                    start=True, stop=True)
                ins.then_inc(ada_cols, 1)

            pe.wait_ge(consts, 6)
            pe.wait_ge(vec_in, 16 * 5)
            pe.transpose(TR[0][:, 0:V_ROWS], stage[0:V_ROWS, 0, :], ident[0:V_ROWS, 0:V_ROWS]).then_inc(cols_t, 1)
            for t in range(QB):
                pe.wait_ge(x_in[t], 16)
                for f in range(2):
                    if t:
                        pe.wait_ge(x_e, 2 * t + f - 1)
                    for q in range(4):
                        kt = 4 * f + q
                        ins = pe.transpose(SC[f][:, q * P:(q + 1) * P], xs[t][:, kt * P:(kt + 1) * P],
                                           ident[:, :])
                    ins.then_inc(x_t, 1)

            def first_modulation(i):
                pe.wait_ge(ada0_sum, i + 1)
                bank_, c0 = (TR[0], 4 * i) if i < 4 else (TR[1], 4 * i - 16)
                for q in range(4):
                    ins = pe.matmul(bank_[:, c0 + q:c0 + q + 1], first_acc[i][:, q * P:(q + 1) * P],
                                    ones[:, 0:1], start=True, stop=True)
                return ins

            def taps(l):
                pe.wait_ge(conv_in[l], 16 * 4)
                for j in range(4):
                    ins = pe.transpose(TR[1][:, j * 2 * FFT:(j + 1) * 2 * FFT],
                                       stage[0:2 * FFT, 1 + j, :], ident[0:2 * FFT, 0:2 * FFT])
                ins.then_inc(cols_t, 1)

            taps(0)
            norm(0, 0)
            first_modulation(0)
            first_modulation(1)
            spread(0)
            first_modulation(2)
            pe.wait_ge(cols_r, 2)
            taps(1)
            first_modulation(3).then_inc(ada_cols, 1)
            two_tiles(C_F, T_F, 0)
            for j in range(1, 3):
                bank_free(T_FOX + j)
                product(C_FOX + j, 0, 0, 0, 3 * DT, h_h, h_l, PJ[(T_FOX + j) % 2])
            first_modulation(4)
            first_modulation(5).then_inc(gate_cols, 1)
            pe.wait_ge(cum_ok, 2)
            pe.wait_ge(pc, 10)

            def scores(u, unit, rows, par, b, head=None):
                nc_ = (b + 1) * P
                sc = SC[u % 2][:, 0:nc_]
                pe_wait_used(unit)
                q = slice(b * P, (b + 1) * P)
                for term in range(3):
                    pe.matmul(sc, q_tile(gl if term == 2 else gh, par)[rows, q],
                              k_tile(gl if term == 1 else gh, par)[rows, 0:nc_], start=term == 0, stop=False)
                if head is not None:
                    pe.matmul(sc, sel[:, (bass.ds(head, 1) if not isinstance(head, int) else head), :],
                              cum[:, 0:nc_], start=False, stop=False)
                pe.matmul(SC[u % 2][:, b * P:nc_], ident_b[:, :], mask_b[:, :], start=False, stop=True
                          ).then_inc(score, 1)

            def pe_wait_used(unit):
                if not isinstance(unit, int) or unit >= 2:
                    pe.wait_ge(expd, unit - 1)

            def turn(u, unit, r, bk):
                b = u % QB
                pe.wait_ge(pn, unit + 1)
                tr_free(r)
                for kb in range(b + 1):
                    ins = pe.transpose(TR[bk][:, kb * P:(kb + 1) * P] if u // QB % 2 == 0 else
                                       TR[bk][:, (b - kb) * P:(b - kb + 1) * P],
                                       prob[u % 4][:, kb * P:(kb + 1) * P], ident[:, :])
                ins.then_inc(tr_r, 1)

            def tr_free(r):
                if not isinstance(r, int) or r >= 2:
                    pe.wait_ge(tr_lo, r - 1)

            def weighted(h, r_last):
                pe.wait_ge(tr_lo, r_last + 1)
                for kb in range(QB):
                    o = pt_off(h, kb, kb)
                    n = S - kb * P
                    for term in range(3):
                        ins = pe.matmul(OV[h][:, kb * P:S], v_all(gl if term == 2 else gh)[:, kb * P:(kb + 1) * P],
                                        (gl if term == 1 else gh)[:, o:o + n],
                                        start=kb == 0 and term == 0, stop=kb == QB - 1 and term == 2)
                ins.then_inc(pv, 1)

            def fox_step(i, s, fill):
                j, u = s // 8, s % 8
                R = i * (2 * FOX_TR) + R_FOX
                n0 = C_FOX + 3 * (j + 1)
                t0 = i * 6 + (T_FOX + 3 * (j + 1))
                if fill:
                    for w in range(3):
                        lo, hi = max(9 * u, 24 * w), min(9 * u + 9, 24 * (w + 1))
                        if lo >= hi:
                            continue
                        if lo == 24 * w:
                            bank_free(t0 + w)
                        product(n0 + w, i, 6, lo - 24 * w, hi - 24 * w, h_h, h_l, PJ[pbank(w, 1 - j)])
                if s < 16:
                    if u == 0:
                        pe.wait_ge(ev_d, t0 - 1)
                    scores(s, i * 16 + (U_FOX + s), slice(u // QB * HD, u // QB * HD + HD), j, u % QB,
                           i * 4 + s // QB)
                v = turned_unit(i, s)
                if v is not None and v < 16:
                    r = FOX_TR * (v // 8) + tr_at(v % 8)
                    turn(v, i * 16 + (U_FOX + v), R + r, r % 2)
                h = done_head(i, s)
                if u % QB == 2 and h is not None:
                    weighted(h % 2, R + (FOX_TR * (h // 2) + tr_at(h % 2 * QB + 3)))
                if s < 16 and u == 2:
                    pe.wait_ge(ev_d, t0)
                    for q in range(QB):
                        ins = pe.transpose(TR[(FOX_TR * j + 1) % 2][:, q * P:(q + 1) * P],
                                           vT[:, q * P:(q + 1) * P], ident[:, :])
                    ins.then_inc(tr_r, 1)

            for s in range(16):
                fox_step(0, s, True)
            last = PAIRS // 2 - 1
            with pe.Fori(1, last) as i:
                for s in range(16):
                    fox_step(i, s, True)
            for s in range(20):
                fox_step(last, s, s < 8)

            def dense(C, T, heads_done):
                def step(i, j):
                    bank_free(i * 2 + (T + j))
                    product(C + j, i, 2, 0, 3 * DT, lambda kt: tile(gh, kt), lambda kt: tile(gl, kt),
                            PJ[(T + j) % 2])
                pe.wait_ge(o_lo, heads_done)
                with pe.Fori(0, DT // 2) as i:
                    for j in range(2):
                        step(i, j)

            def mlp(l):
                def up(i, js):
                    for j in js:
                        bank_free(i * 4 + (T_UP[l] + j))
                        product(C_UP[l] + j, i, 4, 0, 3 * DT, h_h, h_l, PJ[(T_UP[l] + j) % 2])

                two_tiles(C_UP[l], T_UP[l], DT * (2 * l + 1))
                up(0, (2, 3))
                with pe.Fori(1, FFT // 2) as i:
                    up(i, range(4))
                with pe.Fori(0, DT // 2) as i:
                    for j in range(6):
                        k0 = sum(DOWN_K[:j % 3])
                        if j % 3 == 0:
                            bank_free(i * 2 + (T_DOWN[l] + j // 3))
                        pe.wait_ge(g_lo, FFT * l + k0 + DOWN_K[j % 3])
                        product(C_DOWN[l] + j, i, 6, 0, 3 * DOWN_K[j % 3], lambda kt: tile(gh, k0 + kt),
                                lambda kt: tile(gl, k0 + kt), PJ[(T_DOWN[l] + j // 3) % 2],
                                start=j % 3 == 0, stop=j % 3 == 2)

            modulation(1)
            dense(C_FOXO, T_FOXO, HEADS)
            norm(1, 0)
            spread(1)
            mlp(0)
            norm(2, 0)
            modulation(2)
            spread(2)
            two_tiles(C_MA, T_MA, DT * 2)
            for j in range(2, QRT + KVRT + 1):
                bank_free(T_MA + j)
                product(C_MA + j, 0, 0, 0, 3 * DT, h_h, h_l, PJ[(T_MA + j) % 2])
                if j == QRT:
                    norm(N_CQ, 1)
            spread(N_CQ)
            pe.wait_ge(dev, N_CQ + 1)
            norm(N_CKV, 2)
            spread(N_CKV)

            def uq_h(kt):
                return hh[:, kt, :]

            def uq_l(kt):
                return hl[:, kt, :]

            def ukv_h(kt):
                return hh[:, QRT + kt, :]

            def ukv_l(kt):
                return hl[:, QRT + kt, :]

            pe.wait_ge(cn_lo, QRT + KVRT)
            bank_free(T_MLA)
            product(C_MLA, 0, 0, 0, 3 * QRT, uq_h, uq_l, PJ[T_MLA % 2])
            bank_free(T_MLA + 1)
            product(C_MLA + 1, 0, 0, 0, 3 * KVRT, ukv_h, ukv_l, PJ[(T_MLA + 1) % 2])

            def mla_step(t, s, fill):
                j, b = s // QB, s % QB
                R = t * (2 * MLA_TR) + R_MLA
                n0 = C_MLA + 2 * (j + 1)
                t0 = t * 4 + (T_MLA + 2 * (j + 1))
                if fill:
                    for w, (a, e, rh, rl) in enumerate(((0, 9, uq_h, uq_l), (9, 15, ukv_h, ukv_l))):
                        lo, hi = max(6 * b, a), min(6 * b + 6, e)
                        if lo >= hi:
                            continue
                        if lo == a:
                            bank_free(t0 + w)
                        product(n0 + w, t, 4, lo - a, hi - a, rh, rl, PJ[(T_MLA + w) % 2])
                if s < 8:
                    if b == 0:
                        pe.wait_ge(ev_d, t0)
                    scores(s, t * 8 + (U_MLA + s), slice(0, MQ), j, b)
                v = turned_unit(t, s)
                if v is not None and v < 8:
                    r = MLA_TR * (v // QB) + tr_at(v % QB)
                    turn(v, t * 8 + (U_MLA + v), R + r, (R_MLA + r) % 2)
                h = done_head(t, s)
                if b == 2 and h is not None:
                    weighted(h % 2, R + (MLA_TR * h + tr_at(3)))
                if s < 8 and b == 2:
                    for q in range(QB):
                        ins = pe.transpose(TR[(R_MLA + MLA_TR * j + 1) % 2][:, q * HD:(q + 1) * HD],
                                           vT[0:HD, q * P:(q + 1) * P], ident[0:HD, 0:HD])
                    ins.then_inc(tr_r, 1)

            for s in range(8):
                mla_step(0, s, True)
            last = HEADS // 2 - 1
            with pe.Fori(1, last) as t:
                for s in range(8):
                    mla_step(t, s, True)
            for s in range(12):
                mla_step(last, s, s < QB)
            modulation(3)
            dense(C_MLAO, T_MLAO, 2 * HEADS)
            norm(5, 0)
            spread(5)
            mlp(1)
            norm(6, 0)
            spread(6)
            for f in range(2):
                pe.wait_ge(fin, 4 * (f + 1))
                for t in range(QB):
                    if 4 * f + t >= 2:
                        pe.wait_ge(fin_e, 4 * f + t - 1)
                    for q in range(4):
                        ins = pe.transpose(SC[t % 2][:, q * P:(q + 1) * P], xT[:, 4 * f + q, t * P:(t + 1) * P],
                                           ident[:, :])
                    ins.then_inc(fin_t, 1)


_INS = ['x', 'c', 'ada_w', 'ada_b', 'fox_w_in', 'fox_b_f', 'fox_w_o', 'mla_w_a', 'mla_g_q', 'mla_g_kv',
        'mla_w_uq', 'mla_w_ukv', 'mla_w_o', 'ffn_w_in', 'ffn_conv_w', 'ffn_conv_b', 'ffn_w_out', 'final_g']


def rope_table():
    freq = np.float32(10000.0) ** (-np.arange(0, ROPE, 2, dtype=np.float32) / np.float32(ROPE))
    ang = (np.arange(S, dtype=np.float32)[:, None] * freq[None, :].astype(np.float32)).T.astype(np.float64)
    cos, sin = np.cos(ang), np.sin(ang)
    return np.concatenate([cos, cos, -sin, sin]).astype(np.float32)


def kernel(**inputs):
    import concourse.bacc as _bacc
    from concourse.bass_utils import run_bass_kernel_spmd as _run

    nc = _bacc.Bacc("TRN2", target_bir_lowering=False, num_devices=1)
    arrays, args = {}, []
    for name in _INS + ['rope']:
        a = rope_table() if name == 'rope' else np.ascontiguousarray(inputs[name])
        arrays[f"in_{name}_dram"] = a
        args.append(nc.dram_tensor(f"in_{name}_dram", a.shape, mybir.dt.from_np(a.dtype),
                                   kind="ExternalInput").ap())
    args.append(nc.dram_tensor("out_0_dram", (1, S, D), F32, kind="ExternalOutput").ap())
    build(nc, *args)
    r = _run(nc, [arrays], core_ids=[0])
    return r.results[0]["out_0_dram"]
```
